# Optimizing a Trainium2 kernel written in Bass

```python
import math
import jax, jax.numpy as jnp
from jax import lax
import numpy as np

D_MODEL = 1024
BATCH = 1
SEQ = 1024
DEPTH = 1
DEC_BATCH = 8
DEC_SEQ = 16
PAST_LEN = 2048

CHUNK = 64
SB_HEAD_DIM = 64
SB_DIM = D_MODEL // 2
SB_HEADS = SB_DIM // SB_HEAD_DIM
SB_SCALE = SB_HEAD_DIM ** -0.5
Q_BLOCK = 128
CONV_DIM = D_MODEL // 2
CONV_K = 31
N_GROUPS = 4
EXPERTS_PER_GROUP = 4
N_EXPERTS = N_GROUPS * EXPERTS_PER_GROUP
TOP_K = 2
EXPERT_DFF = D_MODEL // 4
LN_EPS = 1e-5
DEEPNORM_ALPHA = (2.0 * DEPTH) ** 0.25
DEEPNORM_BETA = (8.0 * DEPTH) ** -0.25
IN_DIM = 3 * SB_DIM + 2 * CONV_DIM

kernel_name = "stickbreak_conformer_hmoe_stream_step"

def layer_norm(x, g, b):
    xf = x.astype(jnp.float32)
    mu = jnp.mean(xf, axis=-1, keepdims=True)
    var = jnp.mean(jnp.square(xf - mu), axis=-1, keepdims=True)
    y = (xf - mu) * lax.rsqrt(var + LN_EPS) * g.astype(jnp.float32) + b.astype(jnp.float32)
    return y.astype(x.dtype)

def stick_breaking_attention(q, k, v, n_past):
    tq = q.shape[1]
    outs = []
    for qs in range(0, tq, Q_BLOCK):
        qe = min(qs + Q_BLOCK, tq)
        n_keys = n_past + qe
        qb = q[:, qs:qe]
        kb = k[:, :n_keys]
        vb = v[:, :n_keys]
        z = jnp.einsum('bqhd,bkhd->bhqk', qb, kb).astype(jnp.float32) * SB_SCALE
        q_pos = n_past + qs + jnp.arange(qe - qs)
        k_pos = jnp.arange(n_keys)
        mask = k_pos[None, :] < q_pos[:, None]
        log_keep = jnp.where(mask, jax.nn.log_sigmoid(-z), 0.0)
        log_after = lax.cumsum(log_keep, axis=3, reverse=True) - log_keep
        weights = jnp.where(mask, jnp.exp(jax.nn.log_sigmoid(z) + log_after), 0.0)
        outs.append(jnp.einsum('bhqk,bkhd->bqhd', weights.astype(vb.dtype), vb))
    return jnp.concatenate(outs, axis=1)

def causal_depthwise_conv(u_full, conv_w, conv_b):
    out = lax.conv_general_dilated(
        u_full, conv_w[:, None, :].astype(u_full.dtype), window_strides=(1,),
        padding='VALID', dimension_numbers=('NWC', 'WIO', 'NWC'),
        feature_group_count=CONV_DIM)
    return out + conv_b

def hierarchical_moe(h, w_router_group, b_router_group, w_router_expert, b_router_expert,
                     w_expert_gate, w_expert_up, w_expert_down):
    shp = h.shape
    t = h.reshape(-1, D_MODEL)
    n = t.shape[0]
    g_logits = (t @ w_router_group + b_router_group).astype(jnp.float32)
    g_idx = jnp.argmax(g_logits, axis=-1)
    p_group = jnp.take_along_axis(jax.nn.softmax(g_logits, axis=-1), g_idx[:, None], axis=1)
    e_logits = (t @ w_router_expert + b_router_expert).astype(jnp.float32)
    e_logits = e_logits.reshape(n, N_GROUPS, EXPERTS_PER_GROUP)
    e_sel = jnp.take_along_axis(e_logits, g_idx[:, None, None], axis=1)[:, 0]
    top_v, top_i = lax.top_k(e_sel, TOP_K)
    p_expert = jax.nn.softmax(top_v, axis=-1)
    expert_id = g_idx[:, None] * EXPERTS_PER_GROUP + top_i
    combine = jnp.sum(jax.nn.one_hot(expert_id, N_EXPERTS, dtype=jnp.float32)
                      * (p_group * p_expert)[..., None], axis=1).astype(t.dtype)
    y = jnp.zeros_like(t)
    for e in range(N_EXPERTS):
        hid = jax.nn.silu(t @ w_expert_gate[e]) * (t @ w_expert_up[e])
        y = y + combine[:, e:e + 1] * (hid @ w_expert_down[e])
    return y.reshape(shp)

def encoder_layer(x, k_hist, v_hist, conv_hist,
                  w_in, w_branch_attn, w_branch_conv, conv_w, conv_b, conv_ln_g, conv_ln_b,
                  w_gate, b_gate, w_out, ln1_g, ln1_b,
                  w_router_group, b_router_group, w_router_expert, b_router_expert,
                  w_expert_gate, w_expert_up, w_expert_down, ln2_g, ln2_b):
    bsz, tlen, _ = x.shape
    proj = x @ w_in
    q, k, v, glu_val, glu_gate = jnp.split(
        proj, [SB_DIM, 2 * SB_DIM, 3 * SB_DIM, 3 * SB_DIM + CONV_DIM], axis=-1)
    q = q.reshape(bsz, tlen, SB_HEADS, SB_HEAD_DIM)
    k = k.reshape(bsz, tlen, SB_HEADS, SB_HEAD_DIM)
    v = v.reshape(bsz, tlen, SB_HEADS, SB_HEAD_DIM)
    k_all = jnp.concatenate([k_hist, k], axis=1)
    v_all = jnp.concatenate([v_hist, v], axis=1)
    attn = stick_breaking_attention(q, k_all, v_all, k_hist.shape[1])
    branch_a = attn.reshape(bsz, tlen, SB_DIM) @ w_branch_attn
    u = glu_val * jax.nn.sigmoid(glu_gate)
    u_full = jnp.concatenate([conv_hist, u], axis=1)
    c = causal_depthwise_conv(u_full, conv_w, conv_b)
    c = jax.nn.silu(layer_norm(c, conv_ln_g, conv_ln_b))
    branch_b = c @ w_branch_conv
    gates = jax.nn.sigmoid(x @ w_gate + b_gate)
    g_a, g_b = jnp.split(gates, 2, axis=-1)
    mixed = (g_a * branch_a + g_b * branch_b) @ w_out
    h = layer_norm(DEEPNORM_ALPHA * x + mixed, ln1_g, ln1_b)
    ff = hierarchical_moe(h, w_router_group, b_router_group, w_router_expert, b_router_expert,
                          w_expert_gate, w_expert_up, w_expert_down)
    y = layer_norm(DEEPNORM_ALPHA * h + ff, ln2_g, ln2_b)
    return y, k, v, u_full[:, -(CONV_K - 1):]

def setup_inputs(seed: int = 0) -> dict:
    key = jax.random.key(seed)
    ks = jax.random.split(key, 32)

    def nrm(k, shape, scale):
        return jax.random.normal(k, shape, jnp.float32) * scale

    d_sc = D_MODEL ** -0.5
    beta = DEEPNORM_BETA
    w_in = jnp.concatenate([
        nrm(ks[5], (DEPTH, D_MODEL, 2 * SB_DIM), d_sc),
        nrm(ks[6], (DEPTH, D_MODEL, SB_DIM), d_sc * beta),
        nrm(ks[7], (DEPTH, D_MODEL, CONV_DIM), d_sc * beta),
        nrm(ks[8], (DEPTH, D_MODEL, CONV_DIM), d_sc),
    ], axis=-1)
    return {
        "x_prompt": nrm(ks[0], (BATCH, SEQ, D_MODEL), 1.0),
        "x_sample": nrm(ks[1], (DEC_BATCH, DEC_SEQ, D_MODEL), 1.0),
        "cache_k": nrm(ks[2], (DEPTH, DEC_BATCH, PAST_LEN, SB_HEADS, SB_HEAD_DIM), 1.0),
        "cache_v": nrm(ks[3], (DEPTH, DEC_BATCH, PAST_LEN, SB_HEADS, SB_HEAD_DIM), beta),
        "state_conv": nrm(ks[4], (DEPTH, DEC_BATCH, CONV_K - 1, CONV_DIM), 0.5 * beta),
        "w_in": w_in,
        "w_branch_attn": nrm(ks[9], (DEPTH, SB_DIM, D_MODEL), SB_DIM ** -0.5 * beta),
        "w_branch_conv": nrm(ks[10], (DEPTH, CONV_DIM, D_MODEL), CONV_DIM ** -0.5 * beta),
        "conv_w": nrm(ks[11], (DEPTH, CONV_K, CONV_DIM), CONV_K ** -0.5),
        "conv_b": nrm(ks[12], (DEPTH, CONV_DIM), 0.02),
        "conv_ln_g": 1.0 + nrm(ks[13], (DEPTH, CONV_DIM), 0.05),
        "conv_ln_b": nrm(ks[14], (DEPTH, CONV_DIM), 0.02),
        "w_gate": nrm(ks[15], (DEPTH, D_MODEL, 2 * D_MODEL), d_sc),
        "b_gate": nrm(ks[16], (DEPTH, 2 * D_MODEL), 0.02),
        "w_out": nrm(ks[17], (DEPTH, D_MODEL, D_MODEL), d_sc * beta),
        "ln1_g": 1.0 + nrm(ks[18], (DEPTH, D_MODEL), 0.05),
        "ln1_b": nrm(ks[19], (DEPTH, D_MODEL), 0.02),
        "w_router_group": nrm(ks[20], (DEPTH, D_MODEL, N_GROUPS), d_sc),
        "b_router_group": nrm(ks[21], (DEPTH, N_GROUPS), 0.01),
        "w_router_expert": nrm(ks[22], (DEPTH, D_MODEL, N_EXPERTS), d_sc),
        "b_router_expert": nrm(ks[23], (DEPTH, N_EXPERTS), 0.01),
        "w_expert_gate": nrm(ks[24], (DEPTH, N_EXPERTS, D_MODEL, EXPERT_DFF), d_sc * beta),
        "w_expert_up": nrm(ks[25], (DEPTH, N_EXPERTS, D_MODEL, EXPERT_DFF), d_sc * beta),
        "w_expert_down": nrm(ks[26], (DEPTH, N_EXPERTS, EXPERT_DFF, D_MODEL), EXPERT_DFF ** -0.5 * beta),
        "ln2_g": 1.0 + nrm(ks[27], (DEPTH, D_MODEL), 0.05),
        "ln2_b": nrm(ks[28], (DEPTH, D_MODEL), 0.02),
    }

def reference(x_prompt, x_sample, cache_k, cache_v, state_conv,
              w_in, w_branch_attn, w_branch_conv, conv_w, conv_b, conv_ln_g, conv_ln_b,
              w_gate, b_gate, w_out, ln1_g, ln1_b,
              w_router_group, b_router_group, w_router_expert, b_router_expert,
              w_expert_gate, w_expert_up, w_expert_down, ln2_g, ln2_b):
    h_p = x_prompt
    h_s = x_sample
    k_p_list, v_p_list, c_p_list = [], [], []
    k_s_list, v_s_list, c_s_list = [], [], []
    bsz = x_prompt.shape[0]
    for l in range(DEPTH):
        lw = (w_in[l], w_branch_attn[l], w_branch_conv[l], conv_w[l], conv_b[l],
              conv_ln_g[l], conv_ln_b[l], w_gate[l], b_gate[l], w_out[l], ln1_g[l], ln1_b[l],
              w_router_group[l], b_router_group[l], w_router_expert[l], b_router_expert[l],
              w_expert_gate[l], w_expert_up[l], w_expert_down[l], ln2_g[l], ln2_b[l])
        empty_kv = jnp.zeros((bsz, 0, SB_HEADS, SB_HEAD_DIM), h_p.dtype)
        conv_pad = jnp.zeros((bsz, CONV_K - 1, CONV_DIM), h_p.dtype)
        h_p, k_p, v_p, c_p = encoder_layer(h_p, empty_kv, empty_kv, conv_pad, *lw)
        h_s, k_s, v_s, c_s = encoder_layer(h_s, cache_k[l], cache_v[l], state_conv[l], *lw)
        k_p_list.append(k_p)
        v_p_list.append(v_p)
        c_p_list.append(c_p)
        k_s_list.append(k_s)
        v_s_list.append(v_s)
        c_s_list.append(c_s)
    return (h_p, h_s,
            jnp.stack(k_p_list), jnp.stack(v_p_list), jnp.stack(c_p_list),
            jnp.stack(k_s_list), jnp.stack(v_s_list), jnp.stack(c_s_list))


_drawn_inputs = setup_inputs


def setup_inputs(seed=0):
    import zlib

    import numpy as np

    out = dict(_drawn_inputs(seed))
    spreads = {}
    factors = {'cache_k': 7.84,
     'cache_v': 3.268,
     'conv_b': 8.0,
     'conv_ln_g': 8.0,
     'conv_ln_b': 33.889,
     'b_gate': 8.0,
     'ln1_b': 2.77,
     'b_router_group': 64.0,
     'b_router_expert': 64.0,
     'ln2_b': 2.741}
    for name, (base, spread) in spreads.items():
        noise = np.random.default_rng([zlib.crc32(name.encode()), seed]).standard_normal(out[name].shape)
        drawn = base * np.exp(spread * noise) if base else spread * noise
        out[name] = __import__('jax').numpy.asarray(drawn.astype(out[name].dtype))
    for name, factor in factors.items():
        out[name] = (out[name] * factor).astype(out[name].dtype)
    return out
```

```python
from contextlib import ExitStack

import concourse.bass as bass
from concourse import mybir

P = 128
D = 1024
KD = D // P
NPR = 1024
NB, NST = 8, 16
NSA = NB * NST
T = NPR + NSA
NT = T // P
TH = T // 3
C = 4
HD = 64
PAST = 2048
HALF = PAST // 2
CK = 31
HIST = CK - 1
USW = HIST + NST
E, G, EG = 16, 4, 4
F = 256
MT = (2 * T + E * (P - 1)) // P
ALPHA = 2.0 ** 0.25
EPS = 1e-5
SCALE = HD ** -0.5
NEG = -1e30
DVE_TAPS = 28
KB = 1024
BASE = 16512

F32 = mybir.dt.float32
F32R = mybir.dt.float32r
BF16 = mybir.dt.bfloat16
I32 = mybir.dt.int32
ALU = mybir.AluOpType
ACT = mybir.ActivationFunctionType
AX = mybir.AxisListType

K_ID, K_TRI, K_ONE, K_CM, K_SM = 0, 128, 256, 384, 512
K_THR = K_SM + NB * P
K_TILE = K_THR + NT
K_FIRST = K_TILE + MT
K_TOK = K_FIRST + EG
KW = K_TOK + 1

ITEMS = ([("d", 0, 1), ("d", 0, 0)] + [("p", t, h) for t in (7, 0, 5, 2) for h in (0, 1)]
         + [("d", 1, 1), ("d", 1, 0)] + [("p", t, h) for t in (6, 1, 4, 3) for h in (0, 1)])
NI = len(ITEMS)
ROUNDS = 4


def width(item):
    return HALF + P * item[2] if item[0] == "d" else P * (item[1] + 1)


def groups(item):
    nb = width(item) // P
    return [range(g, min(g + 4, nb)) for g in range(0, nb, 4)]


GRP0 = [sum(len(groups(x)) for x in ITEMS[:m]) for m in range(NI + 1)]
NGRP = GRP0[NI]
RT_GEXP, RT_DV, RT_RANK = 6, 20, 24 + NT


NTAP = DVE_TAPS + CK + 1


def tap_no(k, sample):
    if k >= DVE_TAPS:
        return DVE_TAPS + k if sample else None
    return 2 * k + sample


def later(t, n):
    return not isinstance(t, int) or t >= n


DEC = [m for m, x in enumerate(ITEMS) if x[0] == "d"]
TAIL_X = range(DEC[-1] + 2, DEC[-1] + 8)
TAIL_A = range(DEC[-1] + 3, DEC[-1] + 9, 2)
DEC_OLD = [m for m in DEC if ITEMS[m][2] == 0]


def encoder_layer(nc, a):
    ctx = ExitStack()
    with ctx:
        def at(name, shape, dt, kb, b=0):
            return nc.alloc_sbuf_tensor_at(name, shape, dt, offset=BASE + int(kb * KB) + b)

        def sem(name):
            return ctx.enter_context(nc.semaphore(name))

        bank = [ctx.enter_context(nc.psum_tensor(f"bank{i}", [P, 512], F32)) for i in range(3)]
        zb = [ctx.enter_context(nc.psum_tensor(f"zb{i}", [P, 1024], F32)) for i in range(2)]
        bank7 = ctx.enter_context(nc.psum_tensor("bank7", [P, 512], F32))

        cn_sum = [zb[0][:, 0:TH], zb[0][:, 512:512 + TH], zb[1][:, 0:TH]]

        ident = at("ident", [P, P], F32, 203)
        tri = at("tri", [P, P], F32, 203.5)
        ones = at("ones", [P, P], F32, 204)
        ident_b = at("ident_b", [P, P], BF16, 204.5)
        cmask = at("cmask", [P, P], BF16, 204.75)
        smask = at("smask", [P, NB, P], BF16, 205)
        cw = at("cw", [P, C, 32], F32, 207)
        cwc = at("cwc", [P, 32], F32, 207.5)
        lngb = at("lngb", [P, 2, C], F32, 207.5, 128)
        bg = at("bg", [P, 16], F32, 207.5, 160)
        x_hi = at("x_hi", [P, KD, T], F32R, 0)
        x_lo = at("x_lo", [P, KD, T], F32R, 36)
        x_raw = at("x_raw", [P, KD, T], F32, 72)
        qT = at("qT", [P, C, T], F32, 72)
        kT = at("kT", [P, C, T], F32, 90)
        v_p = at("v_p", [P, NPR // P, 512], F32, 108)
        v_s = at("v_s", [P, 512], F32, 124)
        cT = at("cT", [P, C, T], F32, 126)
        mask_raw = at("mask_raw", [P, P * (1 + NB)], F32, 126)
        w_hi = [at(f"w_hi{s}", [P, D], F32R, 144 + 8 * s) for s in range(3)]
        w_lo = [at(f"w_lo{s}", [P, D], F32R, 148 + 8 * s) for s in range(3)]
        w_raw = [at(f"w_raw{s}", [P, D], F32, 168 + 4 * s) for s in range(3)]
        zero = at("zero", [P, 512], F32, 180)
        u = at("u", [P, HIST + NPR + NB * USW], F32, 182)
        u_s = u[:, HIST + NPR:].rearrange("p (b w) -> p b w", w=USW)
        sg = at("sg", [P, T], F32, 182, 5696)
        vT = at("vT", [P, T], F32, 182, 10304)
        pacc = at("pacc", [P, NPR], F32, 182, 14912)
        k_in = [at(f"k_in{s}", [P, 4, HALF], F32, 16 * s) for s in range(2)]
        v_in = [at(f"v_in{s}", [P, HALF // P, 512], F32, 32 + 16 * s) for s in range(2)]
        q_z = at("q_z", [P, 2, NPR], F32, 64)
        keep = [at(f"keep{s}", [P, HALF + P + 1], F32, 144, 4640 * s) for s in range(2)]
        sig = [at(f"sig{s}", [P, HALF + P], F32, 144, 9280 + 4608 * s) for s in range(2)]
        wT = [at(f"wT{s}", [P, 9, P], F32, 144, 18496 + 4608 * s) for s in range(2)]
        v_z = at("v_z", [P, NPR // P, P], F32, 172)
        q_d = [at(f"q_d{s}", [P, 4, 32], F32, 176 + 0.5 * s) for s in range(2)]
        carry = at("carry", [P, 1], F32, 177)
        av_sb = at("av_sb", [P, P], F32, 177.25)
        attnT = at("attnT", [P, C, T], F32, 182)
        a_hi = at("a_hi", [P, C, T], F32R, 72)
        a_lo = at("a_lo", [P, C, T], F32R, 90)
        x_raw2 = [at(f"x_raw2{s}", [P, T], F32, 108, 4608 * s) for s in range(3)]
        c_hi = at("c_hi", [P, C, T], F32R, 108)
        c_lo = at("c_lo", [P, C, T], F32R, 126)
        sq = at("sq", [P, C, TH], F32, 117)
        rstd_c = at("rstd_c", [P, T], F32, 182, 3 * 4608)
        sg_a = at("sg_a", [P, T], F32, 182)
        sg_b = at("sg_b", [P, T], F32, 182, 4608)
        m_sb = at("m_sb", [P, T], F32, 182, 9216)
        wo_hi = at("wo_hi", [P, KD, D], F32R, 0)
        wo_lo = at("wo_lo", [P, KD, D], F32R, 32)
        m_raw = [at(f"m_raw{s}", [P, KD, P], F32, 64 + 4 * s) for s in range(2)]
        m_hi = [at(f"m_hi{s}", [P, KD, P], F32R, 72 + 4 * s) for s in range(2)]
        m_lo = [at(f"m_lo{s}", [P, KD, P], F32R, 80 + 4 * s) for s in range(2)]
        x_n = [at(f"x_n{s}", [P, D], F32, 88 + 4 * s) for s in range(2)]
        r = [at(f"r{s}", [P, D], F32, 96 + 4 * s) for s in range(2)]
        ln1 = at("ln1", [P, 2, D], F32, 104)
        hT = [at(f"hT{s}", [P, KD, P], F32, 112 + 4 * s) for s in range(2)]
        h = at("h", [P, NT, D], F32, 120)
        RTB = 156
        place = [0]

        def small(name, shape, dt=F32):
            n = 4
            for x in shape[1:]:
                n *= x
            place[0] += (n + 31) // 32 * 32
            return at(name, shape, dt, RTB, place[0] - (n + 31) // 32 * 32)

        st = [small(f"st{s}", [P, 12]) for s in range(3)]
        mv = [small(f"mv{s}", [P, 2]) for s in range(3)]
        sd = [small(f"sd{s}", [P, 2]) for s in range(3)]
        rs = [small(f"rs{s}", [P, 2]) for s in range(3)]
        w_r = small("w_r", [P, KD, 20])
        b_r = small("b_r", [P, 20])
        rc = small("rc", [P, KW - K_THR])
        logit = small("logit", [P, NT, 20])
        gmx = small("gmx", [P, NT])
        ge = small("ge", [P, NT, 4])
        gs = small("gs", [P, NT])
        ga = small("ga", [P, NT, 4])
        gm = small("gm", [P, NT])
        goh = small("goh", [P, NT, 4])
        em = small("em", [P, NT, 4, 4])
        es = small("es", [P, NT, 4])
        v1 = small("v1", [P, NT])
        v2 = small("v2", [P, NT])
        oh = [small(f"oh{s}", [P, NT, 4]) for s in range(2)]
        dv = small("dv", [P, NT])
        wt = small("wt", [P, 2, NT])
        oe = [small(f"oe{s}", [P, NT, 16]) for s in range(2)]
        mm_ = small("mm_", [P, NT, 16])
        pre = small("pre", [P, NT + 1, 16])
        tl = small("tl", [P, 16])
        tl9 = small("tl9", [P, 16, NT])
        inc_ = small("inc_", [P, 16])
        base = small("base", [P, 16])
        pos_e = small("pos_e", [P, NT, 16])
        pos_f = small("pos_f", [P, 2, NT])
        pos_i = small("pos_i", [P, 2, NT], I32)
        eq = small("eq", [P, MT, 16])
        et = small("et", [P, MT])
        eti = small("eti", [P, MT], I32)
        assert place[0] <= 12 * KB + 3 * KB, place
        w_x = [at(f"w_x{s}", [P, 6144], F32, 24 * s) for s in range(3)]
        hs = [at(f"hs{s}", [P, D], F32, 72 + 4 * s) for s in range(3)]
        hsT = [at(f"hsT{s}", [P, KD, P], F32, 84 + 4 * s) for s in range(3)]
        sil = [at(f"sil{s}", [P, F], F32, 96 + s) for s in range(3)]
        hid = [at(f"hid{s}", [P, F], F32, 99 + s) for s in range(3)]
        hidT = [at(f"hidT{s}", [P, 2, P], F32, 102 + s) for s in range(3)]
        y_sb = [at(f"y_sb{s}", [P, D], F32, 105 + 4 * s) for s in range(3)]
        ln2 = at("ln2", [P, 2, D], F32, 172)
        y0 = [at(f"y0{s}", [P, D], F32, 4 * s) for s in range(3)]
        y1 = [at(f"y1{s}", [P, D], F32, 12 + 4 * s) for s in range(3)]
        ac = [at(f"ac{s}", [P, D], F32, 24 + 4 * s) for s in range(3)]

        mT_d = nc.dram_tensor("mT_d", (C * 2, P, T), F32, kind="Internal").ap()
        hs_d = nc.dram_tensor("hs_d", (MT * P, D), F32, kind="Internal").ap()
        ys_d = nc.dram_tensor("ys_d", (MT * P, D), F32, kind="Internal").ap()

        s_x = [sem(f"x_landed{i}") for i in range(4)]
        s_const = sem("const_landed")
        s_mask = sem("masks_landed")
        s_w = [sem(f"w_landed{i}") for i in range(3)]
        s_hist = sem("history_landed")
        s_cout = sem("conv_state_stored")
        s_zero = sem("zero_rows_stored")
        s_kv_out = sem("kv_stored")
        s_k = [sem(f"k_landed{i}") for i in range(2)]
        s_v = [sem(f"v_landed{i}") for i in range(2)]
        s_x2 = [sem(f"x_again_landed{i}") for i in range(3)]
        s_m_out = sem("mixed_stored")
        s_wo = [sem(f"wo_landed{i}") for i in range(3)]
        s_m_in = [sem(f"mixed_landed{i}") for i in range(2)]
        s_xn = [sem(f"x_rows_landed{i}") for i in range(2)]
        s_ln1 = sem("out_const_landed")
        s_scat = sem("rows_scattered")
        s_wx = [sem(f"expert_landed{i}") for i in range(3)]
        s_hs = [sem(f"rows_landed{i}") for i in range(3)]
        s_ys = [sem(f"expert_rows_stored{i}") for i in range(3)]
        s_ln2 = sem("ln2_landed")
        s_y0 = [sem(f"y0_gathered{i}") for i in range(3)]
        s_y1 = [sem(f"y1_gathered{i}") for i in range(3)]
        s_y = [sem(f"y_stored{i}") for i in range(3)]
        s_apart = [sem(f"apart{i}") for i in range(4)]
        e_mask = sem("masks_ready")
        e_xhi, e_xlo = sem("x_hi_ready"), sem("x_lo_ready")
        e_whi, e_wlo = sem("w_hi_ready"), sem("w_lo_ready")
        e_proj = sem("proj_done")
        e_free = [sem(f"bank_free{n}") for n in range(3)]
        e_vtr, e_vtr_free = sem("v_transposed"), sem("v_rows_ready")
        e_cw = sem("taps_staged")
        e_tap = sem("conv_tap_done")
        e_ptap = sem("pool_tap_done")
        e_pconv = sem("pool_conv_done")
        e_zero = sem("zero_ready")
        e_idb = sem("ident_b_ready")
        e_qd, e_qz, e_vz, e_stage0 = sem("q_d_staged"), sem("q_z_staged"), sem("v_z_staged"), sem("stage_zeroed")
        e_qk, e_sig, e_scan, e_w = sem("z_ready"), sem("sigmoids_ready"), sem("scan_done"), sem("weights_ready")
        e_tr, e_wt, e_av, e_ae = sem("weights_transposed"), sem("wT_ready"), sem("av_done"), sem("attn_stored")
        e_bnd = sem("boundary_ready")
        e_avt, e_dec = sem("stream_transposed"), sem("stream_stored")
        e_ahi, e_alo = sem("attn_hi_ready"), sem("attn_lo_ready")
        e_xhi2, e_xlo2 = sem("x_hi_again"), sem("x_lo_again")
        e_s1, e_cen, e_sq, e_s2 = sem("mean_summed"), sem("centred"), sem("squared"), sem("squares_summed")
        e_var, e_std, e_rstd, e_xhat = sem("var_ready"), sem("std_ready"), sem("rstd_ready"), sem("xhat_ready")
        e_cn, e_chi, e_clo = sem("swish_ready"), sem("c_hi_ready"), sem("c_lo_ready")
        e_w2hi, e_w2lo, e_proj2 = sem("w2_hi_ready"), sem("w2_lo_ready"), sem("mix_proj_done")
        e_free2 = [sem(f"mix_bank_free{n}") for n in range(3)]
        e_mb, e_m = sem("branches_gated"), sem("mixed_ready")
        e_wohi, e_wolo = sem("wo_hi_ready"), sem("wo_lo_ready")
        e_mhi, e_mlo = sem("m_hi_ready"), sem("m_lo_ready")
        e_out, e_r, e_std1, e_rs1 = sem("out_done"), sem("residual_ready"), sem("std1_ready"), sem("rstd1_ready")
        e_st, e_rcp, e_hh = sem("stats_step"), sem("reciprocal_ready"), sem("h_stored")
        e_n1, e_g1, e_h = sem("normed_ready"), sem("scaled_ready"), sem("h_ready")
        e_htr, e_hT, e_lg, e_lgs = sem("h_transposed"), sem("hT_ready"), sem("logits_done"), sem("logits_stored")
        e_rt, e_rt_act, e_rank, e_pos, e_te = (sem("route_step"), sem("route_exp"), sem("ranks_done"),
                                              sem("positions_ready"), sem("tile_experts_ready"))
        e_gs = sem("route_gexp")
        e_t, e_hsTa, e_hsTv = sem("rows_transposed"), sem("hsT_low_ready"), sem("hsT_high_ready")
        e_gu, e_sil, e_hid, e_t2, e_hidT = (sem("gate_up_done"), sem("silu_ready"), sem("hidden_ready"),
                                           sem("hidden_transposed"), sem("hidT_ready"))
        e_dn, e_yv, e_ya = sem("down_done"), sem("y_low_ready"), sem("y_high_ready")
        e_c0, e_c1, e_c2, e_cst, e_cstd, e_crs, e_cn2, e_cg, e_y = (
            sem("y0_weighted"), sem("y1_added"), sem("residual2_ready"), sem("stats2_step"), sem("std2_ready"),
            sem("rstd2_ready"), sem("normed2_ready"), sem("scaled2_ready"), sem("y_ready"))

        ds = bass.ds

        def apart(e):
            e.sem_inc({nc.scalar: s_apart[0], nc.vector: s_apart[1], nc.gpsimd: s_apart[2], nc.sync: s_apart[3]}[e], 1)

        block = ctx.enter_context(nc.Block())

        SLOT = [0, 1, 0, 1, 2]
        NJ = 5
        PREV = [-3, -2, 0, 1, -1]

        def landed(j, c):
            return 16 * (c + 1) if j == 4 else 16 * (2 * c + (1 if j < 2 else 2))

        def thirds(n):
            return slice(TH * n, TH * (n + 1))

        @block.sync
        def _(e):
            for i in range(4):
                e.dma_start(x_raw[:, 2 * i:2 * i + 2, :], a["xT"][:, 2 * i:2 * i + 2, :]).then_inc(s_x[i], 16)
            e.dma_start(w_raw[0][:, :], a["w_in"][0]).then_inc(s_w[0], 16)
            e.dma_start(w_raw[1][:, :], a["w_in"][1]).then_inc(s_w[1], 16)
            e.dma_start(ident[:, :], a["consts"][:, K_ID:K_ID + P]).then_inc(s_const, 16)
            e.dma_start(tri[:, :], a["consts"][:, K_TRI:K_TRI + P]).then_inc(s_const, 16)
            e.dma_start(ones[:, :], a["consts"][:, K_ONE:K_ONE + P]).then_inc(s_const, 16)
            e.dma_start(cw[:, :, :], a["conv"]).then_inc(s_const, 16)
            e.dma_start(lngb[:, :, :], a["conv_ln"]).then_inc(s_const, 16)
            e.dma_start(bg[:, :], a["b_gate"]).then_inc(s_const, 16)
            e.dma_start(mask_raw[:, :], a["consts"][:, K_CM:K_CM + P * (1 + NB)]).then_inc(s_mask, 16)
            e.wait_ge(e_zero, 1)

            def load_round(c, first):
                for j in range(first, NJ):
                    e.wait_ge(e_whi, c * NJ + (NJ + PREV[j] + 1))
                    e.wait_ge(e_wlo, c * NJ + (NJ + PREV[j] + 1))
                    e.dma_start(w_raw[SLOT[j]][:, :], a["w_in"][ds(c * NJ + j, 1), :, :].rearrange(
                        "a p n -> p (a n)")).then_inc(s_w[SLOT[j]], 16)

            def zero_rows(i, n):
                e.dma_start(hs_d.rearrange("(p r) (h n) -> p r h n", p=P, h=2)[:, ds(i, 1), n, :].rearrange(
                    "p r n -> p (r n)"), zero[:, :]).then_inc(s_zero, 16)

            load_round(0, 2)
            with e.Fori(1, C) as c:
                load_round(c, 0)
                for i in range(MT // 3):
                    zero_rows(c * (MT // 3) + (i - MT // 3), 0)
                    zero_rows(c * (MT // 3) + (i - MT // 3), 1)

            e.wait_ge(e_proj, 15 + 15 * C)

            def load_half(rd, i, stream, half, first=False):
                s = i % 2
                before = DEC[(i + 2) % 4] + (0 if i >= 2 else -NI)
                if not first:
                    e.wait_ge(e_qk, rd * NI + before + 1)
                    apart(e)
                e.dma_start(k_in[s][:, :, :], a["cache_k"][ds(rd * 2 + stream, 1), half, :, :].rearrange(
                    "a p n -> p (a n)").rearrange("p (c n) -> p c n", c=4)).then_inc(s_k[s], 16)
                if not first:
                    e.wait_ge(e_av, rd * NI + before + 1)
                e.dma_start(v_in[s][:, :, :], a["cache_v"][ds(rd * 2 + stream, 1), half, :, :].rearrange(
                    "a p n -> p (a n)").rearrange("p (c n) -> p c n", n=512)).then_inc(s_v[s], 16)

            load_half(0, 0, 0, 1, first=True)
            load_half(0, 1, 0, 0, first=True)
            e.wait_ge(e_free[0], NJ * C)
            e.wait_ge(e_free[1], NJ * C)
            e.wait_ge(e_free[2], NJ * C)
            e.wait_ge(e_vtr_free, 3 * C)
            e.dma_start(a["k_out"], kT[:, :, :]).then_inc(s_kv_out, 16)
            e.dma_start(a["v_out"][0:NPR, :].rearrange("(b p) n -> p b n", p=P), v_p[:, :, :]).then_inc(s_kv_out, 16)
            e.dma_start(a["v_out"][NPR:T, :], v_s[:, :]).then_inc(s_kv_out, 16)
            with e.Fori(0, ROUNDS - 1) as rd:
                load_half(rd, 2, 1, 1)
                load_half(rd, 3, 1, 0)
                load_half(rd + 1, 0, 0, 1)
                load_half(rd + 1, 1, 0, 0)
            load_half(ROUNDS - 1, 2, 1, 1)
            load_half(ROUNDS - 1, 3, 1, 0)

            def load_mix(c, j):
                e.dma_start(w_raw[j][:, :], a["w_mix"][ds(c * 3 + j, 1), :, :].rearrange("a p n -> p (a n)")).then_inc(s_w[j], 16)

            e.wait_ge(s_kv_out, 48)
            e.wait_ge(e_vz, ROUNDS)
            for k in range(KD):
                if k >= 3:
                    e.wait_ge(e_xhi2, k - 2)
                    e.wait_ge(e_xlo2, k - 2)
                e.dma_start(x_raw2[k % 3][:, :], a["xT"][:, k, :]).then_inc(s_x2[k % 3], 16)
            e.wait_ge(e_av, NI * ROUNDS)
            for j in range(3):
                load_mix(0, j)
            with e.Fori(1, C * 2) as c:
                for j in range(3):
                    e.wait_ge(e_w2hi, c * 3 + (j - 2))
                    e.wait_ge(e_w2lo, c * 3 + (j - 2))
                    load_mix(c, j)

            def load_wo(k):
                e.dma_start(w_raw[k % 3][:, :], a["w_out"][k]).then_inc(s_wo[k % 3], 16)

            def load_tile(t, s):
                e.dma_start(m_raw[s][:, :, :], mT_d[:, :, ds(t * P, P)].rearrange("k p n -> p k n")).then_inc(s_m_in[s], 16)
                e.dma_start(x_n[s][:, :], a["x_rows"][ds(t * P, P), :]).then_inc(s_xn[s], 16)

            e.wait_ge(e_w2hi, 3 * 2 * C)
            e.wait_ge(e_w2lo, 3 * 2 * C)
            for k in range(3):
                load_wo(k)
            e.wait_ge(e_proj2, 12 * 2 * C)
            e.dma_start(ln1[:, :, :], a["ln1"]).then_inc(s_ln1, 16)
            e.dma_start(w_r[:, :, :], a["w_router"]).then_inc(s_ln1, 16)
            e.dma_start(b_r[:, :], a["b_router"]).then_inc(s_ln1, 16)
            e.dma_start(rc[:, :], a["consts"][:, K_THR:KW]).then_inc(s_ln1, 16)
            for k in range(3, KD):
                e.wait_ge(e_wohi, k - 2)
                e.wait_ge(e_wolo, k - 2)
                load_wo(k)
            e.wait_ge(s_m_out, 16 * 2 * C)
            load_tile(0, 0)
            load_tile(1, 1)
            with e.Fori(0, 3) as i:
                for s in range(2):
                    e.wait_ge(e_mlo, i * 2 + (s + 1))
                    e.wait_ge(e_r, i * 2 + (s + 1))
                    load_tile(i * 2 + (s + 2), s)
            e.wait_ge(e_mlo, 7)
            e.wait_ge(e_r, 7)
            load_tile(8, 0)
            e.wait_ge(e_wohi, KD)
            e.wait_ge(e_wolo, KD)
            e.dma_start(ln2[:, :, :], a["ln2"]).then_inc(s_ln2, 16)

            def load_rows(i, s):
                e.dma_start(hs[s][:, :], hs_d[ds(i * P, P), :]).then_inc(s_hs[s], 16)

            def load_expert(i, s):
                x = e.value_load(eti[0:1, ds(i, 1)], min_val=0, max_val=E - 1)
                e.dma_start(w_x[s][:, :], a["w_exp"][ds(x, 1), :, :].rearrange("a p n -> p (a n)")).then_inc(s_wx[s], 16)

            def store_rows(i, s):
                e.wait_ge(e_yv, i + 1)
                e.wait_ge(e_ya, i + 1)
                e.dma_start(ys_d[ds(i * P, P), :], y_sb[s][:, :]).then_inc(s_ys[s], 16)

            e.wait_ge(e_te, 1)
            e.wait_ge(e_out, NT)
            for s in range(3):
                load_expert(s, s)
            e.wait_ge(s_scat, 16 * 2 * NT)
            for s in range(3):
                load_rows(s, s)
            with e.Fori(0, MT // 3 - 1) as i:
                for s in range(3):
                    e.wait_ge(e_t, i * 3 + (s + 1))
                    load_rows(i * 3 + (s + 3), s)
                    e.wait_ge(e_dn, i * 3 + (s + 1))
                    load_expert(i * 3 + (s + 3), s)
                    store_rows(i * 3 + s, s)
            for s in range(3):
                store_rows(MT - 3 + s, s)
            for s in range(3):
                e.wait_ge(s_ys[s], 16 * (MT // 3))

            with e.Fori(0, NT // 3) as i:
                for s in range(3):
                    e.wait_ge(e_y, i * 3 + (s + 1))
                    e.dma_start(a["y_out"][ds(i * (3 * P) + s * P, P), :], ac[s][:, :]).then_inc(s_y[s], 16)
            for s in range(3):
                e.wait_ge(s_y[s], 16 * (NT // 3))
            e.wait_ge(s_cout, 32 * C)

        @block.tensor
        def _(e):
            def split_product(outs, w_parts, x_parts, start, stop):
                whi, wlo = w_parts
                xhi, xlo = x_parts
                e.matmul(outs, whi, xhi, start=start, stop=False)
                e.matmul(outs, whi, xlo, start=False, stop=False)
                return e.matmul(outs, wlo, xhi, start=False, stop=stop)

            e.sem_inc(e_proj, 15)
            e.wait_ge(s_const, 96)
            e.wait_ge(e_xlo, 4)
            with e.Fori(0, C) as c:
                for j in range(NJ):
                    s = SLOT[j]
                    e.wait_ge(e_wlo, c * NJ + (NJ + j + 1))
                    for n in range(3):
                        e.wait_ge(e_free[n], c * NJ + j)
                        for k in range(KD):
                            m = split_product(bank[n][:, 0:TH],
                                              (w_hi[s][:, k * P:(k + 1) * P], w_lo[s][:, k * P:(k + 1) * P]),
                                              (x_hi[:, k, thirds(n)], x_lo[:, k, thirds(n)]), k == 0, k == KD - 1)
                        m.then_inc(e_proj, 1)
                    if j == 3:
                        for n in range(3):
                            e.wait_ge(e_free[n], c * NJ + 3)
                        e.wait_ge(e_vtr_free, c * 3)
                        for b in range(NT):
                            tgt = zb[0][:, 128 * b:128 * (b + 1)] if b < 8 else zb[1][:, 0:128]
                            m = e.transpose(tgt, vT[:, b * P:(b + 1) * P], ident[:, :])
                            if b in (3, 7, 8):
                                m.then_inc(e_vtr, 1)

            def scores(rd, m):
                item = ITEMS[m % NI]
                m0 = m % NI
                z = zb[m % 2]
                if m >= 2:
                    e.wait_ge(e_sig, rd * NI + (m - 1))
                if item[0] == "d":
                    i = DEC.index(m0)
                    up = m // NI
                    e.wait_ge(s_k[i % 2], rd * 32 + 16 * (2 * up + i // 2 + 1))
                    e.wait_ge(e_qd, rd * 2 + (2 * up + item[1] + 1))
                    if item[2] == 1:
                        nz = bank[0][:, 0:P]
                        if rd is not None and (m >= NI or item[1] or later(rd, 1)):
                            e.wait_ge(e_dec, rd * 2 + (2 * up + item[1]))
                        e.matmul(nz, ident_b[:, :], smask[:, ds(rd * 2 + (2 * up + item[1]), 1), :].rearrange(
                            "p a n -> p (a n)"), start=True, stop=False, skip_group_check=True)
                        for p in range(4):
                            e.matmul(bank[0][32 * p:32 * p + 32, 0:P], q_d[item[1]][:, p, :], kT[:, p, NPR:T],
                                     start=False, stop=True, skip_group_check=True)
                    for n in range(2):
                        for p in range(4):
                            mm = e.matmul(z[32 * p:32 * p + 32, 512 * n:512 * n + 512], q_d[item[1]][:, p, :],
                                          k_in[i % 2][:, p, 512 * n:512 * n + 512], start=True, stop=True)
                else:
                    _, t, hh = item
                    w = width(item)
                    e.wait_ge(e_qz, rd + (1 + m // NI))
                    for lo in range(0, w, 512):
                        hi = min(lo + 512, w)
                        mm = e.matmul(z[:, lo:hi], q_z[:, hh, t * P:(t + 1) * P],
                                      kT[:, ds(rd + m // NI, 1), lo:hi].rearrange("p a n -> p (a n)"),
                                      start=True, stop=hi < w, skip_group_check=True)
                    mm = e.matmul(z[:, w - P:w], ident_b[:, :], cmask[:, :], start=False, stop=True,
                                  skip_group_check=True)
                mm.then_inc(e_qk, 1)

            def transposes(rd, m):
                item = ITEMS[m]
                off = HALF + P - width(item)
                e.wait_ge(e_w, rd * NI + (m + 1))
                for g, blocks in enumerate(groups(item)):
                    n = GRP0[m] + g
                    e.wait_ge(e_wt, rd * NGRP + (n - 1 if n >= 2 else 0))
                    for b in blocks:
                        mm = e.transpose(bank[1 + n % 2][:, P * (b % 4):P * (b % 4 + 1)],
                                         sig[m % 2][:, off + b * P:off + (b + 1) * P], ident[:, :])
                    mm.then_inc(e_tr, 1)

            def values(rd, m):
                item = ITEMS[m]
                nb = width(item) // P
                if m or later(rd, 1):
                    e.wait_ge(e_ae, rd * NI + m)
                e.wait_ge(e_wt, rd * NGRP + GRP0[m + 1])
                if item[0] == "d":
                    i = DEC.index(m)
                    e.wait_ge(s_v[i % 2], rd * 32 + 16 * (i // 2 + 1))
                    for b in range(nb):
                        for p in range(4):
                            rhs = v_in[i % 2][:, b, P * p:P * (p + 1)] if b < 8 else v_s[:, P * p:P * (p + 1)]
                            mm = e.matmul(bank7[32 * p:32 * p + 32, 0:P], wT[m % 2][:, b, 32 * p:32 * p + 32], rhs,
                                          start=b == 0 and item[2] == 1, stop=b == nb - 1 and item[2] == 0,
                                          skip_group_check=True)
                else:
                    _, t, hh = item
                    e.wait_ge(e_vz, rd + 1)
                    for b in range(nb):
                        mm = e.matmul(bank7[HD * hh:HD * hh + HD, 0:P], v_z[:, b, HD * hh:HD * hh + HD],
                                      wT[m % 2][:, b, :], start=(b == 0), stop=(b == nb - 1))
                mm.then_inc(e_av, 1)

            def stream_transpose(rd, m):
                e.wait_ge(e_ae, rd * NI + (m + 1))
                e.transpose(bank[0][:, P:2 * P], av_sb[:, :], ident[:, :]).then_inc(e_avt, 1)

            def att_round(rd, last):
                for m in range(NI):
                    transposes(rd, m)
                    if m - 1 in DEC_OLD:
                        stream_transpose(rd, m - 1)
                    if m + 2 < NI or not last:
                        scores(rd, m + 2)
                    values(rd, m)

            for n in range(3):
                e.wait_ge(e_free[n], NJ * C)
            e.wait_ge(e_vtr_free, 3 * C)
            e.wait_ge(e_mask, 2)
            e.wait_ge(e_idb, 1)
            scores(0, 0)
            scores(0, 1)
            with e.Fori(0, ROUNDS - 1) as rd:
                att_round(rd, False)
            att_round(ROUNDS - 1, True)

            def channel_sums(signal, step=None):
                for n in range(3):
                    if step is not None:
                        e.wait_ge(step, n + 1)
                    for c in range(C):
                        m = e.matmul(cn_sum[n], ones[:, :], cT[:, c, thirds(n)] if step is None else sq[:, c, :],
                                     start=c == 0, stop=c == C - 1)
                    m.then_inc(signal, 1)

            e.wait_ge(e_sig, NI * ROUNDS)
            channel_sums(e_s1)

            def mix(c):
                for j in range(4):
                    s = min(j, 2)
                    if j < 3:
                        e.wait_ge(e_w2lo, c * 3 + (s + 1))
                    if j == 2:
                        e.wait_ge(e_alo, C)
                    if j == 3:
                        e.wait_ge(e_clo, C)
                    for n in range(3):
                        if j or later(c, 1):
                            e.wait_ge(e_free2[n], c * 4 + j)
                        for k in range(KD if j < 2 else 4):
                            kk = k + 4 * (j == 3)
                            rhs = ((x_hi, x_lo), (x_hi, x_lo), (a_hi, a_lo), (c_hi, c_lo))[j]
                            m = split_product(bank[n][:, 0:TH],
                                              (w_hi[s][:, kk * P:(kk + 1) * P], w_lo[s][:, kk * P:(kk + 1) * P]),
                                              (rhs[0][:, k, thirds(n)], rhs[1][:, k, thirds(n)]),
                                              k == 0, k == (KD if j < 2 else 4) - 1)
                        m.then_inc(e_proj2, 1)
                    if not later(c, 1) and j == 0:
                        channel_sums(e_s2, e_sq)

            e.wait_ge(e_wt, NGRP * ROUNDS)
            e.wait_ge(e_dec, 2 * ROUNDS)
            e.wait_ge(e_xlo2, KD)
            mix(0)
            with e.Fori(1, 2 * C) as c:
                mix(c)

            def out_tile(t, s, first=False):
                e.wait_ge(e_mlo, t + 1)
                if later(t, 2):
                    e.wait_ge(e_r, t - 1)
                for k in range(KD):
                    if first:
                        e.wait_ge(e_wolo, k + 1)
                    for n in range(2):
                        m = split_product(zb[s][:, 512 * n:512 * n + 512], (m_hi[s][:, k, :], m_lo[s][:, k, :]),
                                          (wo_hi[:, k, 512 * n:512 * n + 512], wo_lo[:, k, 512 * n:512 * n + 512]),
                                          k == 0, k == KD - 1)
                m.then_inc(e_out, 1)

            def h_transposes(t, s):
                e.wait_ge(e_h, t + 1)
                if later(t, 1):
                    e.wait_ge(e_hT, t * 2)
                for k in range(KD):
                    m = e.transpose(bank[k // 4][:, P * (k % 4):P * (k % 4 + 1)], r[s][:, k * P:(k + 1) * P], ident[:, :])
                m.then_inc(e_htr, 1)

            def router(t, s):
                e.wait_ge(e_hT, t * 2 + 2)
                if later(t, 1):
                    e.wait_ge(e_lgs, t)
                for k in range(KD):
                    m = e.matmul(bank[2][:, 0:20], hT[s][:, k, :], w_r[:, k, :], start=k == 0, stop=k == KD - 1)
                m.then_inc(e_lg, 1)

            for n in range(3):
                e.wait_ge(e_free2[n], 4 * 2 * C)
            e.wait_ge(s_ln1, 64)
            out_tile(0, 0, first=True)
            out_tile(1, 1)
            h_transposes(0, 0)
            with e.Fori(0, 3) as i:
                for s in range(2):
                    t = i * 2 + (s + 2)
                    out_tile(t, s)
                    router(i * 2 + s, s)
                    h_transposes(i * 2 + (s + 1), 1 - s)
            out_tile(8, 0)
            router(6, 0)
            h_transposes(7, 1)
            router(7, 1)
            h_transposes(8, 0)
            router(8, 0)

            e.wait_ge(e_rt, RT_RANK)
            e.matmul(bank7[:, 0:NT * 16], tri[:, :], mm_[:, :, :].rearrange("p t e -> p (t e)"), start=True, stop=False)
            e.matmul(bank7[:, 0:NT * 16], ones[:, :], pre[:, 0:NT, :].rearrange("p t e -> p (t e)"), start=False, stop=True)
            e.matmul(zb[1][:, 0:16], ones[:, :], pre[:, NT, :], start=True, stop=True).then_inc(e_rank, 1)

            def rows_t(i, s, n=0):
                e.wait_ge(s_hs[s], n * 16 + 16)
                if later(i, 1):
                    e.wait_ge(e_hsTa, i)
                    e.wait_ge(e_hsTv, i)
                for k in range(KD):
                    m = e.transpose(bank[k // 4][:, P * (k % 4):P * (k % 4 + 1)], hs[s][:, k * P:(k + 1) * P], ident[:, :])
                m.then_inc(e_t, 1)

            def gate_up(i, s, n=0):
                e.wait_ge(e_hsTa, i + 1)
                e.wait_ge(e_hsTv, i + 1)
                if later(i, 1):
                    e.wait_ge(e_hid, i)
                e.wait_ge(s_wx[s], n * 16 + 16)
                for k in range(KD):
                    m = e.matmul(bank[2][:, :], hsT[s][:, k, :], w_x[s][:, 512 * k:512 * (k + 1)], start=k == 0, stop=k == KD - 1)
                m.then_inc(e_gu, 1)

            def hidden_t(i, s):
                e.wait_ge(e_hid, i + 1)
                if later(i, 1):
                    e.wait_ge(e_hidT, i)
                for k in range(2):
                    m = e.transpose(bank7[:, P * k:P * (k + 1)], hid[s][:, P * k:P * (k + 1)], ident[:, :])
                m.then_inc(e_t2, 1)

            def down(i, s):
                e.wait_ge(e_hidT, i + 1)
                if later(i, 1):
                    e.wait_ge(e_yv, i)
                    e.wait_ge(e_ya, i)
                for n in range(2):
                    for k in range(2):
                        m = e.matmul(zb[0][:, 512 * n:512 * (n + 1)], hidT[s][:, k, :],
                                     w_x[s][:, 4096 + 1024 * k + 512 * n:4096 + 1024 * k + 512 * (n + 1)],
                                     start=k == 0, stop=k == 1)
                m.then_inc(e_dn, 1)

            e.wait_ge(e_pos, 1)
            rows_t(0, 0)
            gate_up(0, 0)
            rows_t(1, 1)
            hidden_t(0, 0)
            with e.Fori(0, MT // 3 - 1) as i:
                for u_ in range(3):
                    t = i * 3 + (u_ + 1)
                    gate_up(t, (u_ + 1) % 3, i + (u_ + 1) // 3)
                    down(i * 3 + u_, u_)
                    rows_t(i * 3 + (u_ + 2), (u_ + 2) % 3, i + (u_ + 2) // 3)
                    hidden_t(t, (u_ + 1) % 3)
            gate_up(MT - 2, 1, MT // 3 - 1)
            down(MT - 3, 0)
            rows_t(MT - 1, 2, MT // 3 - 1)
            hidden_t(MT - 2, 1)
            gate_up(MT - 1, 2, MT // 3 - 1)
            down(MT - 2, 1)
            hidden_t(MT - 1, 2)
            down(MT - 1, 2)

        @block.scalar
        def _(e):
            e.sem_inc(e_whi, NJ)
            for i in range(4):
                e.wait_ge(s_x[i], 16)
                e.activation(x_hi[:, 2 * i:2 * i + 2, :], x_raw[:, 2 * i:2 * i + 2, :], ACT.Copy).then_inc(e_xhi, 1)

            def split_hi(c, j):
                e.wait_ge(s_w[SLOT[j]], landed(j, c))
                e.wait_ge(e_proj, c * 15 + (15 + 3 * (PREV[j] + 1)))
                e.activation(w_hi[SLOT[j]][:, :], w_raw[SLOT[j]][:, :], ACT.Copy).then_inc(e_whi, 1)

            def round_(c, last):
                for j in range(NJ):
                    if j + 1 < NJ:
                        split_hi(c, j + 1)
                    elif not last:
                        split_hi(c + 1, 0)
                    if j == 3:
                        for n in range(3):
                            e.wait_ge(e_proj, c * 15 + (15 + 3 * j + n + 1))
                            e.activation(qT[:, ds(c, 1), thirds(n)].rearrange("p a n -> p (a n)"), bank[n][:, 0:TH],
                                         ACT.Copy).then_inc(e_free[n], 1)
                        for n in range(3):
                            e.wait_ge(e_vtr, c * 3 + (n + 1))
                            if n < 2:
                                src = zb[0][:, 512 * n:512 * (n + 1)].rearrange("p (b n) -> p b n", n=P)
                                dst = v_p[:, 4 * n:4 * n + 4, ds(c * P, P)]
                            else:
                                src, dst = zb[1][:, 0:P], v_s[:, ds(c * P, P)]
                            e.activation(dst, src, ACT.Copy).then_inc(e_vtr_free, 1)
                    elif j == 4:
                        for n in range(3):
                            e.wait_ge(e_proj, c * 15 + (15 + 3 * j + n + 1))
                            e.activation(kT[:, ds(c, 1), thirds(n)].rearrange("p a n -> p (a n)"), bank[n][:, 0:TH],
                                         ACT.Copy).then_inc(e_free[n], 1)
                    elif j in (0, 2):
                        if j == 0:
                            e.wait_ge(e_pconv, c)
                        for n in range(3):
                            e.wait_ge(e_proj, c * 15 + (15 + 3 * j + n + 1))
                            e.activation((sg if j == 0 else vT)[:, thirds(n)], bank[n][:, 0:TH],
                                         ACT.Sigmoid if j == 0 else ACT.Copy).then_inc(e_free[n], 1)

            split_hi(0, 0)
            with e.Fori(0, C - 1) as c:
                round_(c, False)
            round_(C - 1, True)

            def sigmoids(rd, m):
                item = ITEMS[m % NI]
                w = width(item)
                off = HALF + P - w
                s = m % 2
                e.wait_ge(e_qk, rd * NI + (m + 1))
                if m >= 2:
                    e.wait_ge(e_w, rd * NI + (m - 1))
                    e.wait_ge(e_tr, rd * NGRP + GRP0[m - 1])
                parts = [(bank[0][:, 0:P], HALF, P)] if item[0] == "d" and item[2] == 1 else []
                wz = HALF if item[0] == "d" else w
                parts.append((zb[s][:, 0:wz], off, wz))
                for src, o, n in parts:
                    e.activation(keep[s][:, o:o + n], src, ACT.Sigmoid, scale=-SCALE)
                    i = e.activation(sig[s][:, o:o + n], src, ACT.Sigmoid, scale=SCALE)
                i.then_inc(e_sig, 1)

            def x_again_hi(k):
                e.wait_ge(s_x2[k % 3], 16 * (k // 3 + 1))
                e.activation(x_hi[:, k, :], x_raw2[k % 3][:, :], ACT.Copy).then_inc(e_xhi2, 1)

            def attn_hi(c):
                if c == 0:
                    e.wait_ge(e_qz, ROUNDS)
                e.wait_ge(e_ae, NI * c + NI)
                e.wait_ge(e_dec, 2 * ROUNDS)
                e.activation(a_hi[:, c, :], attnT[:, c, :], ACT.Copy).then_inc(e_ahi, 1)

            def copies(rd, m):
                e.wait_ge(e_av, rd * NI + max(m - 1, 0))
                for g, blocks in enumerate(groups(ITEMS[m])):
                    n = GRP0[m] + g
                    e.wait_ge(e_tr, rd * NGRP + (n + 1))
                    e.activation(wT[m % 2][:, blocks[0]:blocks[-1] + 1, :],
                                 bank[1 + n % 2][:, 0:P * len(blocks)].rearrange("p (b n) -> p b n", n=P),
                                 ACT.Copy).then_inc(e_wt, 1)

            def att_round(rd, last):
                for m in range(NI):
                    if m + 1 < NI or not last:
                        sigmoids(rd, m + 1)
                    copies(rd, m)
                    if last:
                        if m in TAIL_X:
                            x_again_hi(TAIL_X.index(m))
                        if m in TAIL_A:
                            attn_hi(TAIL_A.index(m))

            sigmoids(0, 0)
            with e.Fori(0, ROUNDS - 1) as rd:
                att_round(rd, False)
            att_round(ROUNDS - 1, True)

            W0 = [16 * 2 * C, 16 * 2 * C, 16 * C]

            def split2_hi(c, j, first=False):
                e.wait_ge(s_w[j], c * 16 + (W0[j] + 16))
                if not first:
                    e.wait_ge(e_proj2, c * 12 - (12 - (3, 6, 12)[j]))
                e.activation(w_hi[j][:, :], w_raw[j][:, :], ACT.Copy).then_inc(e_w2hi, 1)

            def gate(c, j):
                for n in range(3):
                    e.wait_ge(e_proj2, c * 12 + (3 * j + n + 1))
                    apart(e)
                    e.activation((sg_a, sg_b)[j][:, thirds(n)], bank[n][:, 0:TH], ACT.Sigmoid,
                                 bias=bg[:, ds(c * 2 + j, 1)]).then_inc(e_free2[n], 1)

            def mix(c, last):
                e.wait_ge(e_m, c)
                for j in range(2):
                    gate(c, j)
                    if not last:
                        split2_hi(c + 1, j)
                if not last:
                    split2_hi(c + 1, 2)

            for k in (6, 7):
                x_again_hi(k)
            attn_hi(3)
            split2_hi(0, 0, first=True)
            split2_hi(0, 1, first=True)
            for n in range(3):
                e.wait_ge(e_cen, n + 1)
                if n == 0:
                    e.wait_ge(e_xlo2, KD)
                else:
                    e.wait_ge(e_s2, n)
                e.activation(sq[:, :, :], cT[:, :, thirds(n)], ACT.Square).then_inc(e_sq, 1)
            split2_hi(0, 2, first=True)
            e.wait_ge(e_alo, C)
            gate(0, 0)
            split2_hi(1, 0)
            for n in range(3):
                e.wait_ge(e_var, n + 1)
                e.activation(rstd_c[:, thirds(n)], rstd_c[:, thirds(n)], ACT.Sqrt).then_inc(e_std, 1)
            for c in range(C):
                e.wait_ge(e_xhat, c + 1)
                e.activation(cT[:, c, :], cT[:, c, :], ACT.Silu, scale=lngb[:, 0, c:c + 1],
                             bias=lngb[:, 1, c:c + 1]).then_inc(e_cn, 1)
                e.wait_ge(e_cn, c + 1)
                e.activation(c_hi[:, c, :], cT[:, c, :], ACT.Copy).then_inc(e_chi, 1)
            gate(0, 1)
            split2_hi(1, 1)
            split2_hi(1, 2)
            with e.Fori(1, 2 * C - 1) as c:
                mix(c, False)
            mix(2 * C - 1, True)

            e.wait_ge(e_proj2, 12 * 2 * C)
            for k in range(KD):
                e.wait_ge(s_wo[k % 3], 16 * (k // 3 + 1))
                e.activation(wo_hi[:, k, :], w_raw[k % 3][:, :], ACT.Copy).then_inc(e_wohi, 1)

            def split_m(t, s, i=0):
                e.wait_ge(s_m_in[s], i * 16 + 16)
                if later(t, 2):
                    e.wait_ge(e_out, t - 1)
                e.activation(m_hi[s][:, :, :], m_raw[s][:, :, :], ACT.Copy).then_inc(e_mhi, 1)

            def std_and_norm(t, s):
                e.wait_ge(e_st, t * 3 + 3)
                e.activation(sd[s][:, 0:1], mv[s][:, 1:2], ACT.Sqrt).then_inc(e_std1, 1)
                e.wait_ge(e_rs1, t + 1)
                e.activation(r[s][:, :], r[s][:, :], ACT.Identity, scale=rs[s][:, 0:1], bias=rs[s][:, 1:2]).then_inc(e_n1, 1)

            def copy_hT(t, s):
                e.wait_ge(e_htr, t + 1)
                for k in range(2):
                    e.activation(hT[s][:, 4 * k:4 * k + 4, :], bank[k][:, :].rearrange("p (b n) -> p b n", n=P),
                                 ACT.Copy).then_inc(e_hT, 1)

            split_m(0, 0)
            split_m(1, 1)
            std_and_norm(0, 0)
            with e.Fori(0, 3) as i:
                for s in range(2):
                    split_m(i * 2 + (s + 2), s, i + 1)
                    std_and_norm(i * 2 + (s + 1), 1 - s)
                    copy_hT(i * 2 + s, s)
            split_m(8, 0, 4)
            std_and_norm(7, 1)
            copy_hT(6, 0)
            std_and_norm(8, 0)
            copy_hT(7, 1)
            copy_hT(8, 0)

            e.wait_ge(e_rt, RT_GEXP)
            e.activation(ge[:, :, :], ge[:, :, :], ACT.Exp).then_inc(e_gs, 1)
            e.wait_ge(e_rt, RT_DV)
            e.activation(dv[:, :], dv[:, :], ACT.Exp).then_inc(e_rt_act, 1)

            def copy_rows(i, s):
                e.wait_ge(e_t, i + 1)
                if later(i, 3):
                    e.wait_ge(e_gu, i - 2)
                e.activation(hsT[s][:, 0:4, :], bank[0][:, :].rearrange("p (b n) -> p b n", n=P), ACT.Copy).then_inc(e_hsTa, 1)

            def silu(i, s):
                e.wait_ge(e_gu, i + 1)
                if later(i, 3):
                    e.wait_ge(e_hid, i - 2)
                e.activation(sil[s][:, :], bank[2][:, 0:F], ACT.Silu).then_inc(e_sil, 1)

            def copy_hidden(i, s):
                e.wait_ge(e_t2, i + 1)
                if later(i, 3):
                    e.wait_ge(e_dn, i - 2)
                e.activation(hidT[s][:, :, :], bank7[:, 0:F].rearrange("p (b n) -> p b n", n=P), ACT.Copy).then_inc(e_hidT, 1)

            def copy_y(i, s, n=0):
                e.wait_ge(e_dn, i + 1)
                if later(i, 3):
                    e.wait_ge(s_ys[s], n * 16)
                e.activation(y_sb[s][:, 512:1024], zb[0][:, 512:1024], ACT.Copy).then_inc(e_ya, 1)

            def moe_step(t, s, nt, ns, y, ys, n=0):
                silu(t, s)
                if y is not None:
                    copy_y(y, ys, n)
                if nt is not None:
                    copy_rows(nt, ns)
                copy_hidden(t, s)

            copy_rows(0, 0)
            moe_step(0, 0, 1, 1, None, 0)
            for t in (1, 2, 3):
                moe_step(t, t % 3, t + 1, (t + 1) % 3, t - 1, (t - 1) % 3, (t - 1) // 3)
            with e.Fori(1, MT // 3 - 1) as i:
                for u_ in range(3):
                    moe_step(i * 3 + (u_ + 1), (u_ + 1) % 3, i * 3 + (u_ + 2), (u_ + 2) % 3, i * 3 + u_, u_, i)
            moe_step(MT - 2, 1, MT - 1, 2, MT - 3, 0, MT // 3 - 1)
            moe_step(MT - 1, 2, None, 0, MT - 2, 1, MT // 3 - 1)
            copy_y(MT - 1, 2, MT // 3 - 1)

            e.wait_ge(e_dn, MT)
            with e.Fori(0, NT // 3) as i:
                for s in range(3):
                    e.wait_ge(s_y0[s], i * 16 + 16)
                    e.wait_ge(s_y[s], i * 16)
                    e.activation(ac[s][:, :], y0[s][:, :], ACT.Copy, scale=wt[:, 0, ds(i * 3 + s, 1)]).then_inc(e_c0, 1)
                    e.wait_ge(e_cst, i * 9 + (s * 3 + 3))
                    e.activation(sd[s][:, 0:1], mv[s][:, 1:2], ACT.Sqrt).then_inc(e_cstd, 1)
                    e.wait_ge(e_crs, i * 3 + (s + 1))
                    e.activation(ac[s][:, :], ac[s][:, :], ACT.Identity, scale=rs[s][:, 0:1], bias=rs[s][:, 1:2]).then_inc(e_cn2, 1)

        @block.vector
        def _(e):
            def tt(out, x, y, op):
                return e.tensor_tensor(out, x, y, op)

            e.sem_inc(e_wlo, NJ)
            e.memset(u[:, 0:HIST], 0.0)
            for i in range(4):
                e.wait_ge(e_xhi, i + 1)
                tt(x_lo[:, 2 * i:2 * i + 2, :], x_raw[:, 2 * i:2 * i + 2, :], x_hi[:, 2 * i:2 * i + 2, :].bitcast(F32),
                   ALU.subtract).then_inc(e_xlo, 1)

            def split_lo(c, j):
                e.wait_ge(e_whi, c * NJ + (NJ + j + 1))
                s = SLOT[j]
                tt(w_lo[s][:, :], w_raw[s][:, :], w_hi[s][:, :].bitcast(F32), ALU.subtract).then_inc(e_wlo, 1)

            def taps(c, lo, hi):
                o = cT[:, ds(c, 1), 0:NPR].rearrange("p a n -> p (a n)")
                os_ = cT[:, ds(c, 1), NPR:T].rearrange("p a (b w) -> p (a b) w", w=NST)
                if lo == 0:
                    e.wait_ge(e_cw, c + 1)
                    e.wait_ge(s_hist, c * 16 + 16)
                for k in range(lo, hi):
                    for out, src, n, before in ((o, u[:, k:k + NPR], tap_no(k, 0), tap_no(k - 1, 0)),
                                                (os_, u_s[:, :, k:k + NST], tap_no(k, 1), tap_no(k - 1, 1))):
                        if n is None:
                            continue
                        if k == 0:
                            i = e.tensor_scalar(out, src, cwc[:, 0:1], cwc[:, CK:CK + 1], ALU.mult, ALU.add)
                        else:
                            e.wait_ge(e_tap, c * NTAP + (before + 1))
                            i = e.scalar_tensor_tensor(out=out, in0=src, scalar=cwc[:, k:k + 1], in1=out,
                                                       op0=ALU.mult, op1=ALU.add)
                        i.then_inc(e_tap, 1)
                if hi == CK:
                    e.wait_ge(e_pconv, c + 1)
                    e.wait_ge(e_tap, c * NTAP + (NTAP - 1))
                    tt(o, o, pacc[:, :], ALU.add).then_inc(e_tap, 1)

            def round_(c, last):
                split_lo(c, 1)
                split_lo(c, 2)
                e.wait_ge(e_pconv, c)
                e.wait_ge(s_cout, c * 32)
                e.wait_ge(e_tap, c * NTAP)
                for n in range(3):
                    e.wait_ge(e_proj, c * 15 + (15 + 3 + n + 1))
                    np_ = TH if n < 2 else NPR - 2 * TH
                    i = tt(u[:, HIST + TH * n:HIST + TH * n + np_], bank[n][:, 0:np_], sg[:, TH * n:TH * n + np_], ALU.mult)
                    if n == 2:
                        i = tt(u_s[:, :, HIST:USW], bank[n][:, np_:TH].rearrange("p (b w) -> p b w", w=NST),
                               sg[:, NPR:T].rearrange("p (b w) -> p b w", w=NST), ALU.mult)
                    i.then_inc(e_free[n], 1)
                e.wait_ge(e_free[2], c * NJ + 2)
                taps(c, 0, 7)
                split_lo(c, 3)
                taps(c, 7, 14)
                split_lo(c, 4)
                taps(c, 14, 24)
                if not last:
                    split_lo(c + 1, 0)
                taps(c, 24, CK)

            split_lo(0, 0)
            e.wait_ge(e_mask, 2)
            with e.Fori(0, C - 1) as c:
                round_(c, False)
            round_(C - 1, True)

            W = HALF + P

            def scan(rd, m):
                item = ITEMS[m % NI]
                s = m % 2
                off = W - width(item)
                old = item[0] == "d" and item[2] == 0
                e.wait_ge(e_sig, rd * NI + (m + 1))
                if old:
                    e.wait_ge(e_w, rd * NI + m)
                    i = e.tensor_copy(keep[s][:, W:W + 1], carry[:, :])
                else:
                    i = e.memset(keep[s][:, W:W + 1], 1.0)
                i.then_inc(e_bnd, 1)
                e.wait_ge(e_bnd, rd * NI + (m + 1))
                rev = keep[s][:, off:W][:, ::-1]
                e.tensor_tensor_scan(rev, rev, rev, carry[:, :] if old else 1.0, ALU.mult, ALU.bypass).then_inc(e_scan, 1)
                e.wait_ge(e_scan, rd * NI + (m + 1))
                if item[0] == "d" and item[2] == 1:
                    e.tensor_copy(carry[:, :], keep[s][:, off:off + 1])
                tt(sig[s][:, off:W], sig[s][:, off:W], keep[s][:, off + 1:W + 1], ALU.mult).then_inc(e_w, 1)

            def store(rd, m):
                item = ITEMS[m]
                if item[0] == "d" and item[2] == 1:
                    e.sem_inc(e_ae, 1)
                    return
                e.wait_ge(e_av, rd * NI + (m + 1))
                if item[0] == "p":
                    _, t, hh = item
                    rows = slice(HD * hh, HD * hh + HD)
                    i = e.tensor_copy(attnT[rows, ds(rd, 1), t * P:(t + 1) * P].rearrange("p a n -> p (a n)"), bank7[rows, 0:P])
                else:
                    i = e.tensor_copy(av_sb[:, :], bank7[:, 0:P])
                i.then_inc(e_ae, 1)

            def store_stream(rd, stream):
                e.wait_ge(e_avt, rd * 2 + (stream + 1))
                av = bank[0][:, P:2 * P].rearrange("p (c w) -> p c w", w=32)
                for hh in range(2):
                    rows = slice(HD * hh, HD * hh + HD)
                    i = e.tensor_copy(attnT[rows, :, ds(rd * (2 * NST) + (NPR + NST * stream), NST)],
                                      av[rows, :, NST * hh:NST * hh + NST])
                i.then_inc(e_dec, 1)

            def x_again_lo(k):
                e.wait_ge(e_xhi2, k + 1)
                tt(x_lo[:, k, :], x_raw2[k % 3][:, :], x_hi[:, k, :].bitcast(F32), ALU.subtract).then_inc(e_xlo2, 1)

            def attn_lo(c):
                e.wait_ge(e_ahi, c + 1)
                tt(a_lo[:, c, :], attnT[:, c, :], a_hi[:, c, :].bitcast(F32), ALU.subtract).then_inc(e_alo, 1)

            def att_round(rd, last):
                for m in range(NI):
                    if m + 1 < NI or not last:
                        scan(rd, m + 1)
                    if m - 1 in DEC_OLD:
                        store_stream(rd, ITEMS[m - 1][1])
                    store(rd, m)
                    if last:
                        if m in TAIL_X:
                            x_again_lo(TAIL_X.index(m))
                        if m in TAIL_A:
                            attn_lo(TAIL_A.index(m))

            e.wait_ge(e_pconv, C)
            e.wait_ge(s_cout, 32 * C)
            e.wait_ge(e_tap, C * NTAP)
            scan(0, 0)
            with e.Fori(0, ROUNDS - 1) as rd:
                att_round(rd, False)
            att_round(ROUNDS - 1, True)

            def split2_lo(c, j):
                e.wait_ge(e_w2hi, c * 3 + (j + 1))
                tt(w_lo[j][:, :], w_raw[j][:, :], w_hi[j][:, :].bitcast(F32), ALU.subtract).then_inc(e_w2lo, 1)

            def mix(c, last, first=False):
                if not last and not first:
                    split2_lo(c + 1, 0)
                if not last:
                    split2_lo(c + 1, 1)
                for j in range(2):
                    for n in range(3):
                        e.wait_ge(e_proj2, c * 12 + (3 * (j + 2) + n + 1))
                        o = (sg_a, sg_b)[j][:, thirds(n)]
                        tt(o, bank[n][:, 0:TH], o, ALU.mult).then_inc(e_free2[n], 1)
                if not last:
                    split2_lo(c + 1, 2)

            for k in (6, 7):
                x_again_lo(k)
            attn_lo(3)
            split2_lo(0, 0)
            split2_lo(0, 1)
            for n in range(3):
                e.wait_ge(e_s1, n + 1)
                for c in range(C):
                    i = e.scalar_tensor_tensor(out=cT[:, c, thirds(n)], in0=cn_sum[n], scalar=-1.0 / 512,
                                               in1=cT[:, c, thirds(n)], op0=ALU.mult, op1=ALU.add)
                i.then_inc(e_cen, 1)
            split2_lo(0, 2)
            for n in range(3):
                e.wait_ge(e_s2, n + 1)
                e.tensor_scalar(rstd_c[:, thirds(n)], cn_sum[n], 1.0 / 512, EPS, ALU.mult, ALU.add).then_inc(e_var, 1)
            e.wait_ge(e_std, 3)
            e.reciprocal(rstd_c[:, :], rstd_c[:, :]).then_inc(e_rstd, 1)
            e.wait_ge(e_rstd, 1)
            for c in range(C):
                tt(cT[:, c, :], cT[:, c, :], rstd_c[:, :], ALU.mult).then_inc(e_xhat, 1)
            split2_lo(1, 0)
            for c in range(C):
                e.wait_ge(e_chi, c + 1)
                tt(c_lo[:, c, :], cT[:, c, :], c_hi[:, c, :].bitcast(F32), ALU.subtract).then_inc(e_clo, 1)
            mix(0, False, first=True)
            with e.Fori(1, 2 * C - 1) as c:
                mix(c, False)
            mix(2 * C - 1, True)

            for k in range(KD):
                e.wait_ge(e_wohi, k + 1)
                tt(wo_lo[:, k, :], w_raw[k % 3][:, :], wo_hi[:, k, :].bitcast(F32), ALU.subtract).then_inc(e_wolo, 1)

            def split_m(t, s):
                e.wait_ge(e_mhi, t + 1)
                tt(m_lo[s][:, :, :], m_raw[s][:, :, :], m_hi[s][:, :, :].bitcast(F32), ALU.subtract).then_inc(e_mlo, 1)

            def stats(x, s, step, n0):
                e.bn_stats(st[s][:, 0:6], x[:, 0:512])
                e.bn_stats(st[s][:, 6:12], x[:, 512:1024]).then_inc(step, 1)
                e.wait_ge(step, n0 + 1)
                apart(e)
                e.bn_aggr(mv[s][:, :], st[s][:, :]).then_inc(step, 1)
                e.wait_ge(step, n0 + 2)
                e.tensor_scalar(mv[s][:, 1:2], mv[s][:, 1:2], EPS, None, ALU.add).then_inc(step, 1)

            def residual(t, s, i=0):
                e.wait_ge(e_out, t + 1)
                e.wait_ge(s_xn[s], i * 16 + 16)
                if later(t, 2):
                    e.wait_ge(e_htr, t - 1)
                    e.wait_ge(e_hh, t - 1)
                e.scalar_tensor_tensor(out=r[s][:, :], in0=x_n[s][:, :], scalar=ALPHA, in1=zb[s][:, :],
                                       op0=ALU.mult, op1=ALU.add).then_inc(e_r, 1)
                e.wait_ge(e_r, t + 1)
                stats(r[s], s, e_st, t * 3)
                e.wait_ge(e_std1, t + 1)
                e.reciprocal(rs[s][:, 0:1], sd[s][:, 0:1]).then_inc(e_rcp, 1)
                e.wait_ge(e_rcp, t + 1)
                e.scalar_tensor_tensor(out=rs[s][:, 1:2], in0=mv[s][:, 0:1], scalar=-1.0, in1=rs[s][:, 0:1],
                                       op0=ALU.mult, op1=ALU.mult).then_inc(e_rs1, 1)
                e.wait_ge(e_n1, t + 1)
                tt(r[s][:, :], r[s][:, :], ln1[:, 0, :], ALU.mult).then_inc(e_g1, 1)

            def store_logits(t):
                e.wait_ge(e_lg, t + 1)
                tt(logit[:, ds(t, 1), :].rearrange("p a n -> p (a n)"), bank[2][:, 0:20], b_r[:, :], ALU.add).then_inc(e_lgs, 1)

            split_m(0, 0)
            split_m(1, 1)
            residual(0, 0)
            with e.Fori(0, 3) as i:
                for s in range(2):
                    split_m(i * 2 + (s + 2), s)
                    residual(i * 2 + (s + 1), 1 - s, i + s)
                    store_logits(i * 2 + s)
            split_m(8, 0)
            residual(7, 1, 3)
            store_logits(6)
            residual(8, 0, 4)
            store_logits(7)
            store_logits(8)

            step = [0]

            def link(i):
                step[0] += 1
                i.then_inc(e_rt, 1)
                e.wait_ge(e_rt, step[0])

            def over(x, n):
                return x.rearrange("p (m o) -> p m o", o=1).to_broadcast([P, x.shape[1], n])

            def first_max(src, mx, score, best, out):
                link(e.tensor_reduce(mx, src, AX.X, ALU.max))
                link(tt(score, src, over(mx, 4), ALU.is_equal))
                link(tt(score, score, rc[:, K_FIRST - K_THR:K_FIRST - K_THR + 4].rearrange("p (o m) -> p o m", o=1)
                        .to_broadcast([P, NT, 4]), ALU.mult))
                link(e.tensor_reduce(best, score, AX.X, ALU.max))
                link(tt(out, score, over(best, 4), ALU.is_equal))

            e.wait_ge(e_lgs, NT)
            lg = logit[:, :, 0:4]
            first_max(lg, gmx[:, :], ga[:, :, :], gm[:, :], goh[:, :, :])
            link(tt(ge[:, :, :], lg, over(gmx[:, :], 4), ALU.subtract))
            assert step[0] == RT_GEXP
            link(tt(em[:, :, :, :], logit[:, :, 4:20].rearrange("p t (g j) -> p t g j", g=4),
                    goh[:, :, :].rearrange("p t (g o) -> p t g o", o=1).to_broadcast([P, NT, 4, 4]), ALU.mult))
            link(e.tensor_reduce(es[:, :, :], em[:, :, :, :].rearrange("p t g j -> p t j g"), AX.X, ALU.add))
            first_max(es[:, :, :], v1[:, :], ga[:, :, :], gm[:, :], oh[0][:, :, :])
            link(e.scalar_tensor_tensor(out=es[:, :, :], in0=oh[0][:, :, :], scalar=NEG, in1=es[:, :, :],
                                        op0=ALU.mult, op1=ALU.add))
            first_max(es[:, :, :], v2[:, :], ga[:, :, :], gm[:, :], oh[1][:, :, :])
            link(tt(dv[:, :], v2[:, :], v1[:, :], ALU.subtract))
            assert step[0] == RT_DV, step
            for k in range(2):
                link(tt(oe[k][:, :, :].rearrange("p t (g j) -> p t g j", g=4),
                        goh[:, :, :].rearrange("p t (g o) -> p t g o", o=1).to_broadcast([P, NT, 4, 4]),
                        oh[k][:, :, :].rearrange("p t (o j) -> p t o j", o=1).to_broadcast([P, NT, 4, 4]), ALU.mult))
            link(tt(mm_[:, :, :], oe[0][:, :, :], oe[1][:, :, :], ALU.add))
            link(e.memset(pre[:, 0, :], 0.0))
            for t in range(NT):
                link(tt(pre[:, t + 1, :], pre[:, t, :], mm_[:, t, :], ALU.add))
            assert step[0] == RT_RANK, step
            e.wait_ge(e_gs, 1)
            link(e.tensor_reduce(gs[:, :], ge[:, :, :], AX.X, ALU.add))
            link(e.reciprocal(gs[:, :], gs[:, :]))
            e.wait_ge(e_rt_act, 1)
            link(e.tensor_scalar(v1[:, :], dv[:, :], 1.0, None, ALU.add))
            link(e.reciprocal(v1[:, :], v1[:, :]))
            link(tt(wt[:, 0, :], v1[:, :], gs[:, :], ALU.mult))
            link(tt(wt[:, 1, :], wt[:, 0, :], dv[:, :], ALU.mult))
            e.wait_ge(e_rank, 1)
            link(tt(tl9[:, :, :], zb[1][:, 0:16].rearrange("p (m o) -> p m o", o=1).to_broadcast([P, 16, NT]),
                    rc[:, 0:NT].rearrange("p (o m) -> p o m", o=1).to_broadcast([P, 16, NT]), ALU.is_gt))
            link(e.tensor_reduce(tl[:, :], tl9[:, :, :], AX.X, ALU.add))
            link(e.tensor_tensor_scan(inc_[:, :], tl[:, :], tl[:, :], 0.0, ALU.add, ALU.bypass))
            link(tt(base[:, :], inc_[:, :], tl[:, :], ALU.subtract))
            link(e.tensor_scalar(base[:, :], base[:, :], float(P), None, ALU.mult))
            link(tt(pos_e[:, :, :], bank7[:, 0:NT * 16].rearrange("p (t m) -> p t m", t=NT),
                    base[:, :].rearrange("p (o m) -> p o m", o=1).to_broadcast([P, NT, 16]), ALU.add))
            for k in range(2):
                link(tt(oe[k][:, :, :], oe[k][:, :, :], pos_e[:, :, :], ALU.mult))
                link(e.tensor_reduce(pos_f[:, k, :], oe[k][:, :, :], AX.X, ALU.add))
            e.tensor_copy(pos_i[:, :, :], pos_f[:, :, :]).then_inc(e_pos, 1)
            link(tt(eq[:, :, :], rc[:, K_TILE - K_THR:K_TILE - K_THR + MT].rearrange("p (m o) -> p m o", o=1)
                    .to_broadcast([P, MT, 16]),
                    inc_[:, :].rearrange("p (o m) -> p o m", o=1).to_broadcast([P, MT, 16]), ALU.is_ge))
            link(e.tensor_reduce(et[:, :], eq[:, :, :], AX.X, ALU.add))
            link(e.tensor_scalar(et[:, :], et[:, :], float(E - 1), None, ALU.min))
            e.tensor_copy(eti[:, :], et[:, :]).then_inc(e_te, 1)

            def copy_rows(i, s):
                e.wait_ge(e_t, i + 1)
                if later(i, 3):
                    e.wait_ge(e_gu, i - 2)
                e.tensor_copy(hsT[s][:, 4:8, :], bank[1][:, :].rearrange("p (b n) -> p b n", n=P)).then_inc(e_hsTv, 1)

            def hidden(i, s):
                e.wait_ge(e_sil, i + 1)
                if later(i, 3):
                    e.wait_ge(e_t2, i - 2)
                tt(hid[s][:, :], sil[s][:, :], bank[2][:, F:2 * F], ALU.mult).then_inc(e_hid, 1)

            def copy_y(i, s, n=0):
                e.wait_ge(e_dn, i + 1)
                if later(i, 3):
                    e.wait_ge(s_ys[s], n * 16)
                e.tensor_copy(y_sb[s][:, 0:512], zb[0][:, 0:512]).then_inc(e_yv, 1)

            def moe_step(t, s, nt, ns, y, ys, n=0):
                hidden(t, s)
                if y is not None:
                    copy_y(y, ys, n)
                if nt is not None:
                    copy_rows(nt, ns)

            copy_rows(0, 0)
            moe_step(0, 0, 1, 1, None, 0)
            for t in (1, 2, 3):
                moe_step(t, t % 3, t + 1, (t + 1) % 3, t - 1, (t - 1) % 3, (t - 1) // 3)
            with e.Fori(1, MT // 3 - 1) as i:
                for u_ in range(3):
                    moe_step(i * 3 + (u_ + 1), (u_ + 1) % 3, i * 3 + (u_ + 2), (u_ + 2) % 3, i * 3 + u_, u_, i)
            moe_step(MT - 2, 1, MT - 1, 2, MT - 3, 0, MT // 3 - 1)
            moe_step(MT - 1, 2, None, 0, MT - 2, 1, MT // 3 - 1)
            copy_y(MT - 1, 2, MT // 3 - 1)

            e.wait_ge(s_ln2, 16)
            with e.Fori(0, NT // 3) as i:
                for s in range(3):
                    t = i * 3 + s
                    e.wait_ge(e_c0, t + 1)
                    e.wait_ge(s_y1[s], i * 16 + 16)
                    e.scalar_tensor_tensor(out=ac[s][:, :], in0=y1[s][:, :], scalar=wt[:, 1, ds(t, 1)], in1=ac[s][:, :],
                                           op0=ALU.mult, op1=ALU.add).then_inc(e_c1, 1)
                    e.wait_ge(e_c1, t + 1)
                    e.scalar_tensor_tensor(out=ac[s][:, :], in0=h[:, ds(t, 1), :].rearrange("p a n -> p (a n)"),
                                           scalar=ALPHA, in1=ac[s][:, :], op0=ALU.mult, op1=ALU.add).then_inc(e_c2, 1)
                    e.wait_ge(e_c2, t + 1)
                    stats(ac[s], s, e_cst, i * 9 + s * 3)
                    e.wait_ge(e_cstd, t + 1)
                    e.reciprocal(rs[s][:, 0:1], sd[s][:, 0:1]).then_inc(e_rcp, 1)
                    e.wait_ge(e_rcp, t + (NT + 1))
                    e.scalar_tensor_tensor(out=rs[s][:, 1:2], in0=mv[s][:, 0:1], scalar=-1.0, in1=rs[s][:, 0:1],
                                           op0=ALU.mult, op1=ALU.mult).then_inc(e_crs, 1)
                    e.wait_ge(e_cn2, t + 1)
                    tt(ac[s][:, :], ac[s][:, :], ln2[:, 0, :], ALU.mult).then_inc(e_cg, 1)

        @block.gpsimd
        def _(e):
            e.memset(zero[:, :], 0.0).then_inc(e_zero, 1)
            e.wait_ge(s_mask, 16)
            e.tensor_copy(cmask[:, :], mask_raw[:, 0:P]).then_inc(e_mask, 1)
            e.tensor_copy(smask[:, :, :], mask_raw[:, P:].rearrange("p (b n) -> p b n", n=P)).then_inc(e_mask, 1)
            e.wait_ge(s_const, 96)
            e.tensor_copy(ident_b[:, :], ident[:, :]).then_inc(e_idb, 1)
            n_p = CK - DVE_TAPS
            NPT = 2 * n_p - 2
            prod = sg[:, 0:NPR]
            with e.Fori(0, C) as c:
                e.wait_ge(e_tap, c * NTAP)
                e.tensor_copy(cwc[:, :], cw[:, ds(c, 1), :].rearrange("p a n -> p (a n)")).then_inc(e_cw, 1)
                e.wait_ge(s_cout, c * 32)
                e.dma_start(u_s[:, :, 0:HIST], a["hist"][ds(c, 1), :, :, :].rearrange("a p b w -> p (a b) w")).then_inc(s_hist, 16)
                e.wait_ge(e_cw, c + 1)
                e.wait_ge(e_free[2], c * NJ + 2)
                e.wait_ge(s_hist, c * 16 + 16)
                e.dma_start(a["conv_out"][ds(c, 1), :, 0, :].rearrange("a p w -> p (a w)"),
                            u[:, NPR:NPR + HIST]).then_inc(s_cout, 16)
                e.dma_start(a["conv_out"][ds(c, 1), :, 1:1 + NB, :].rearrange("a p b w -> p (a b) w"),
                            u_s[:, :, NST:USW]).then_inc(s_cout, 16)
                n = 0
                for k in range(DVE_TAPS, CK):
                    if n:
                        e.wait_ge(e_ptap, c * NPT + n)
                        apart(e)
                    i = e.tensor_scalar(prod if n else pacc[:, :], u[:, k:k + NPR], cwc[:, k:k + 1], None, ALU.mult)
                    i.then_inc(e_ptap, 1)
                    n += 1
                    if n > 1:
                        e.wait_ge(e_ptap, c * NPT + n)
                        apart(e)
                        i = e.tensor_tensor(pacc[:, :], pacc[:, :], prod, ALU.add)
                        i.then_inc(e_ptap if k < CK - 1 else e_pconv, 1)
                        n += 1
                assert n == NPT + 1

            for n in range(3):
                e.wait_ge(e_free[n], NJ * C)
            e.wait_ge(e_proj, 15 + 15 * C)
            e.wait_ge(e_wlo, NJ + NJ * C)
            e.wait_ge(e_vtr_free, 3 * C)
            e.memset(q_z[:, :, :], 0.0).then_inc(e_stage0, 1)
            e.memset(q_d[0][:, :, :], 0.0).then_inc(e_stage0, 1)
            e.memset(q_d[1][:, :, :], 0.0).then_inc(e_stage0, 1)
            e.wait_ge(e_stage0, 3)

            def stage_q_d(rd, a_):
                for hh in range(2):
                    rows = slice(HD * hh, HD * hh + HD)
                    i = e.tensor_copy(q_d[a_][rows, :, NST * hh:NST * hh + NST],
                                      qT[rows, :, ds(rd * (2 * NST) + (NPR + NST * a_), NST)])
                i.then_inc(e_qd, 1)

            def stage_q_z(rd):
                for hh in range(2):
                    rows = slice(HD * hh, HD * hh + HD)
                    i = e.tensor_copy(q_z[rows, hh, :], qT[rows, ds(rd, 1), 0:NPR].rearrange("p a n -> p (a n)"))
                i.then_inc(e_qz, 1)

            def stage_v_z(rd):
                e.wait_ge(e_qz, rd + 1)
                e.tensor_copy(v_z[:, :, :], v_p[:, :, ds(rd * P, P)]).then_inc(e_vz, 1)

            stage_q_d(0, 0)
            stage_q_z(0)
            stage_v_z(0)
            e.wait_ge(e_vz, 1)
            stage_q_d(0, 1)
            with e.Fori(0, ROUNDS - 1) as rd:
                e.wait_ge(e_vz, rd + 1)
                e.wait_ge(e_qk, rd * NI + (DEC[1] + 1))
                stage_q_d(rd + 1, 0)
                e.wait_ge(e_qk, rd * NI + (DEC[3] + 1))
                stage_q_d(rd + 1, 1)
                e.wait_ge(e_qk, rd * NI + NI)
                stage_q_z(rd + 1)
                e.wait_ge(e_av, rd * NI + NI)
                stage_v_z(rd + 1)

            with e.Fori(0, 2 * C) as c:
                for n in range(3):
                    e.wait_ge(e_free2[n], c * 4 + 4)
                e.wait_ge(s_m_out, c * 16)
                e.tensor_tensor(m_sb[:, :], sg_a[:, :], sg_b[:, :], ALU.add).then_inc(e_m, 1)
                e.wait_ge(e_m, c + 1)
                e.dma_start(mT_d[ds(c, 1), :, :].rearrange("a p n -> p (a n)"), m_sb[:, :]).then_inc(s_m_out, 16)

            def add_b(t, s):
                e.wait_ge(e_g1, t + 1)
                e.tensor_tensor(r[s][:, :], r[s][:, :], ln1[:, 1, :], ALU.add).then_inc(e_h, 1)
                e.wait_ge(e_h, t + 1)
                e.tensor_copy(h[:, ds(t, 1), :].rearrange("p a n -> p (a n)"), r[s][:, :]).then_inc(e_hh, 1)

            with e.Fori(0, 4) as i:
                for s in range(2):
                    add_b(i * 2 + s, s)
            add_b(8, 0)

            e.wait_ge(e_pos, 1)
            e.wait_ge(s_zero, 16 * 2 * MT)
            e.wait_ge(e_hh, NT)
            for t in range(NT):
                for k in range(2):
                    e.indirect_dma_start(hs_d[:, :], bass.IndirectOffsetOnAxis(ap=pos_i[:, k, t:t + 1], axis=0),
                                         h[:, t, :], None).then_inc(s_scat, 16)

            def gather(t, s):
                for k, (y, sm) in enumerate(((y0, s_y0), (y1, s_y1))):
                    e.indirect_dma_start(y[s][:, :], None, ys_d[:, :],
                                         bass.IndirectOffsetOnAxis(ap=pos_i[:, k, t:t + 1], axis=0)).then_inc(sm[s], 16)

            def add_b2(t, s):
                e.wait_ge(e_cg, t + 1)
                e.tensor_tensor(ac[s][:, :], ac[s][:, :], ln2[:, 1, :], ALU.add).then_inc(e_y, 1)

            for s in range(3):
                e.wait_ge(s_ys[s], 16 * (MT // 3))
            e.wait_ge(e_dn, MT)
            for t in range(3):
                gather(t, t)
            for t in range(NT):
                add_b2(t, t % 3)
                if t + 3 < NT:
                    gather(t + 3, t % 3)


def _consts(np):
    k = np.zeros((P, KW), np.float32)
    i = np.arange(P)
    k[:, K_ID:K_ID + P] = np.eye(P)
    k[:, K_TRI:K_TRI + P] = i[:, None] < i[None, :]
    k[:, K_ONE:K_ONE + P] = 1
    k[:, K_CM:K_CM + P] = np.where(i[None, :] < i[:, None], 0, NEG)
    b, j = i // NST, i % NST
    for n in range(NB):
        seen = (b[None, :] == n) & (j[None, :] < j[:, None])
        k[:, K_SM + n * P:K_SM + (n + 1) * P] = np.where(seen, 0, NEG)
    k[:, K_THR:K_THR + NT] = P * np.arange(NT)
    k[:, K_TILE:K_TILE + MT] = np.arange(MT)
    k[:, K_FIRST:K_FIRST + EG] = EG - np.arange(EG)
    return k


def kernel(x_prompt, x_sample, cache_k, cache_v, state_conv, w_in, w_branch_attn, w_branch_conv, conv_w, conv_b,
           conv_ln_g, conv_ln_b, w_gate, b_gate, w_out, ln1_g, ln1_b, w_router_group, b_router_group, w_router_expert,
           b_router_expert, w_expert_gate, w_expert_up, w_expert_down, ln2_g, ln2_b):
    import numpy as np
    from concourse import bacc
    from concourse.bass_utils import run_bass_kernel_spmd

    def arr(x):
        return np.asarray(x)

    def chunks(w):
        k, n = w.shape
        return w.reshape(k // P, P, n // P, P).transpose(2, 1, 0, 3).reshape(n // P, P, k)

    def rows(v, n=P):
        return np.broadcast_to(v, (n, *v.shape))

    x_rows = np.concatenate([arr(x_prompt)[0], arr(x_sample).reshape(NSA, D)], 0)
    wi = chunks(arr(w_in)[0]).reshape(5, C, P, D)
    w_in_u = np.stack([wi[4], wi[3], wi[2], wi[0], wi[1]], 1).reshape(5 * C, P, D)
    wg = chunks(arr(w_gate)[0]).reshape(2, 2 * C, P, D)
    wb = np.concatenate([chunks(arr(w_branch_attn)[0]), chunks(arr(w_branch_conv)[0])], 2)
    w_mix = np.stack([wg[0], wg[1], wb], 1).reshape(6 * C, P, D)
    gu = np.concatenate([arr(w_expert_gate)[0], arr(w_expert_up)[0]], 2).reshape(E, KD, P, 2 * F)
    dn = arr(w_expert_down)[0].reshape(E, 2, P, D)
    w_exp = np.concatenate([gu.transpose(0, 2, 1, 3).reshape(E, P, KD * 2 * F),
                            dn.transpose(0, 2, 1, 3).reshape(E, P, 2 * D)], 2)
    conv = np.concatenate([arr(conv_w)[0].T.reshape(C, P, CK), arr(conv_b)[0].reshape(C, P, 1)], 2).transpose(1, 0, 2)
    ins = {
        "xT": x_rows.T.reshape(KD, P, T).transpose(1, 0, 2),
        "x_rows": x_rows,
        "w_in": w_in_u,
        "w_mix": w_mix,
        "w_out": arr(w_out)[0].reshape(KD, P, D),
        "w_exp": w_exp,
        "consts": _consts(np),
        "conv": conv,
        "conv_ln": np.stack([arr(conv_ln_g)[0].reshape(C, P).T, arr(conv_ln_b)[0].reshape(C, P).T], 1),
        "b_gate": arr(b_gate)[0].reshape(2, 2 * C, P).transpose(2, 1, 0).reshape(P, 4 * C),
        "ln1": rows(np.stack([arr(ln1_g)[0], arr(ln1_b)[0]])),
        "ln2": rows(np.stack([arr(ln2_g)[0], arr(ln2_b)[0]])),
        "w_router": np.concatenate([arr(w_router_group)[0], arr(w_router_expert)[0]], 1).reshape(KD, P, 20).transpose(1, 0, 2),
        "b_router": rows(np.concatenate([arr(b_router_group)[0], arr(b_router_expert)[0]])),
        "cache_k": arr(cache_k)[0].reshape(NB, 2, HALF, C, P).transpose(0, 1, 4, 3, 2).reshape(NB, 2, P, C * HALF),
        "cache_v": arr(cache_v)[0].reshape(NB, 2, HALF // P, P, 512).transpose(0, 1, 3, 2, 4).reshape(NB, 2, P, -1),
        "hist": arr(state_conv)[0].reshape(NB, HIST, C, P).transpose(2, 3, 0, 1),
    }
    outs = {
        "y_out": (T, D), "k_out": (P, C, T), "v_out": (T, 512), "conv_out": (C, P, 1 + NB, HIST),
    }
    nc = bacc.Bacc("TRN2", target_bir_lowering=False, num_devices=1)
    a = {}
    for n, x in ins.items():
        ins[n] = np.ascontiguousarray(x)
        a[n] = nc.dram_tensor(n, ins[n].shape, mybir.dt.from_np(ins[n].dtype), kind="ExternalInput").ap()
    for n, shape in outs.items():
        a[n] = nc.dram_tensor(n, shape, F32, kind="ExternalOutput").ap()
    encoder_layer(nc, a)
    got = run_bass_kernel_spmd(nc, [ins], core_ids=[0]).results[0]

    y = got["y_out"]
    k = got["k_out"].transpose(2, 1, 0).reshape(T, 8, HD)
    v = got["v_out"].reshape(T, 8, HD)
    cv = got["conv_out"].transpose(2, 3, 0, 1).reshape(1 + NB, HIST, 512)
    return (y[None, :NPR], y[NPR:].reshape(NB, NST, D),
            k[None, None, :NPR], v[None, None, :NPR], cv[None, :1],
            k[NPR:].reshape(1, NB, NST, 8, HD), v[NPR:].reshape(1, NB, NST, 8, HD), cv[None, 1:])
```

```python
from contextlib import ExitStack

import concourse.bass as bass
from concourse import mybir

P = 128
D = 1024
KD = D // P
NPR = 1024
NB, NST = 8, 16
NSA = NB * NST
T = NPR + NSA
NT = T // P
TH = T // 3
C = 4
HD = 64
PAST = 2048
HALF = PAST // 2
CK = 31
HIST = CK - 1
USW = HIST + NST
E, G, EG = 16, 4, 4
F = 256
MT = (2 * T + E * (P - 1)) // P
ALPHA = 2.0 ** 0.25
EPS = 1e-5
SCALE = HD ** -0.5
NEG = -1e30
DVE_TAPS = 28
KB = 1024
BASE = 16512

F32 = mybir.dt.float32
F32R = mybir.dt.float32r
BF16 = mybir.dt.bfloat16
I32 = mybir.dt.int32
ALU = mybir.AluOpType
ACT = mybir.ActivationFunctionType
AX = mybir.AxisListType

K_ID, K_TRI, K_ONE, K_CM, K_SM = 0, 128, 256, 384, 512
K_THR = K_SM + NB * P
K_TILE = K_THR + NT
K_FIRST = K_TILE + MT + 1
KW = K_FIRST + EG

ITEMS = ([("d", 0, 1), ("d", 0, 0)] + [("p", t, h) for t in (7, 0, 5, 2) for h in (0, 1)]
         + [("d", 1, 1), ("d", 1, 0)] + [("p", t, h) for t in (6, 1, 4, 3) for h in (0, 1)])
NI = len(ITEMS)
ROUNDS = 4


def width(item):
    return HALF + P * item[2] if item[0] == "d" else P * (item[1] + 1)


def groups(item):
    nb = width(item) // P
    return [range(g, min(g + 4, nb)) for g in range(0, nb, 4)]


GRP0 = [sum(len(groups(x)) for x in ITEMS[:m]) for m in range(NI + 1)]
NGRP = GRP0[NI]
RT_GEXP, RT_DV, RT_RANK = 6, 20, 24 + NT


NTAP = DVE_TAPS + CK + 1


def tap_no(k, sample):
    if k >= DVE_TAPS:
        return DVE_TAPS + k if sample else None
    return 2 * k + sample


def later(t, n):
    return not isinstance(t, int) or t >= n


X_PARTS = [0, 2, 5, 7, KD]
DEC = [m for m, x in enumerate(ITEMS) if x[0] == "d"]
TAIL_X = range(DEC[-1] + 2, DEC[-1] + 8)
TAIL_A = range(DEC[-1] + 3, DEC[-1] + 9, 2)
DEC_OLD = [m for m in DEC if ITEMS[m][2] == 0]


def encoder_layer(nc, a):
    ctx = ExitStack()
    with ctx:
        def at(name, shape, dt, kb, b=0):
            return nc.alloc_sbuf_tensor_at(name, shape, dt, offset=BASE + int(kb * KB) + b)

        def sem(name):
            return ctx.enter_context(nc.semaphore(name))

        bank = [ctx.enter_context(nc.psum_tensor(f"bank{i}", [P, 512], F32)) for i in range(3)]
        zb = [ctx.enter_context(nc.psum_tensor(f"zb{i}", [P, 1024], F32)) for i in range(2)]
        bank7 = ctx.enter_context(nc.psum_tensor("bank7", [P, 512], F32))

        cn_sum = [zb[0][:, 0:TH], zb[0][:, 512:512 + TH], zb[1][:, 0:TH]]

        ident = at("ident", [P, P], F32, 203)
        tri = at("tri", [P, P], F32, 203.5)
        ones = at("ones", [P, P], F32, 204)
        ident_b = at("ident_b", [P, P], BF16, 204.5)
        cmask = at("cmask", [P, P], BF16, 204.75)
        smask = at("smask", [P, NB, P], BF16, 205)
        cw = at("cw", [P, C, 32], F32, 207)
        cwc = at("cwc", [P, 32], F32, 207.5)
        lngb = at("lngb", [P, 2, C], F32, 207.5, 128)
        bg = at("bg", [P, 16], F32, 207.5, 160)
        x_hi = at("x_hi", [P, KD, T], F32R, 0)
        x_lo = at("x_lo", [P, KD, T], F32R, 36)
        x_raw = at("x_raw", [P, KD, T], F32, 72)
        qT = at("qT", [P, C, T], F32, 72)
        kT = at("kT", [P, C, T], F32, 90)
        v_p = at("v_p", [P, NPR // P, 512], F32, 108)
        v_s = at("v_s", [P, 512], F32, 124)
        cT = at("cT", [P, C, T], F32, 126)
        mask_raw = at("mask_raw", [P, P * (1 + NB)], F32, 126)
        w_hi = [at(f"w_hi{s}", [P, D], F32R, 144 + 8 * s) for s in range(3)]
        w_lo = [at(f"w_lo{s}", [P, D], F32R, 148 + 8 * s) for s in range(3)]
        w_raw = [at(f"w_raw{s}", [P, D], F32, 168 + 4 * s) for s in range(3)]
        zero = at("zero", [P, 512], F32, 180)
        u = at("u", [P, HIST + NPR + NB * USW], F32, 182)
        u_s = u[:, HIST + NPR:].rearrange("p (b w) -> p b w", w=USW)
        sg = at("sg", [P, T], F32, 182, 5696)
        vT = at("vT", [P, T], F32, 182, 10304)
        pacc = at("pacc", [P, NPR], F32, 182, 14912)
        k_in = [at(f"k_in{s}", [P, 4, HALF], F32, 16 * s) for s in range(2)]
        v_in = [at(f"v_in{s}", [P, HALF // P, 512], F32, 32 + 16 * s) for s in range(2)]
        q_z = at("q_z", [P, 2, NPR], F32, 64)
        keep = [at(f"keep{s}", [P, HALF + P + 1], F32, 144, 4640 * s) for s in range(2)]
        sig = [at(f"sig{s}", [P, HALF + P], F32, 144, 9280 + 4608 * s) for s in range(2)]
        wT = [at(f"wT{s}", [P, 9, P], F32, 144, 18496 + 4608 * s) for s in range(2)]
        v_z = at("v_z", [P, NPR // P, P], F32, 172)
        q_d = [at(f"q_d{s}", [P, 4, 32], F32, 176 + 0.5 * s) for s in range(2)]
        carry = at("carry", [P, 1], F32, 177)
        av_sb = at("av_sb", [P, P], F32, 177.25)
        attnT = at("attnT", [P, C, T], F32, 182)
        a_hi = at("a_hi", [P, C, T], F32R, 72)
        a_lo = at("a_lo", [P, C, T], F32R, 90)
        x_raw2 = [at(f"x_raw2{s}", [P, T], F32, 108, 4608 * s) for s in range(3)]
        c_hi = at("c_hi", [P, C, T], F32R, 108)
        c_lo = at("c_lo", [P, C, T], F32R, 126)
        sq = at("sq", [P, C, TH], F32, 117)
        rstd_c = at("rstd_c", [P, T], F32, 182, 3 * 4608)
        sg_a = at("sg_a", [P, T], F32, 182)
        sg_b = at("sg_b", [P, T], F32, 182, 4608)
        m_sb = at("m_sb", [P, T], F32, 182, 9216)
        wo_hi = at("wo_hi", [P, KD, D], F32R, 0)
        wo_lo = at("wo_lo", [P, KD, D], F32R, 32)
        m_raw = [at(f"m_raw{s}", [P, KD, P], F32, 64 + 4 * s) for s in range(2)]
        m_hi = [at(f"m_hi{s}", [P, KD, P], F32R, 72 + 4 * s) for s in range(2)]
        m_lo = [at(f"m_lo{s}", [P, KD, P], F32R, 80 + 4 * s) for s in range(2)]
        x_n = [at(f"x_n{s}", [P, D], F32, 88 + 4 * s) for s in range(2)]
        r = [at(f"r{s}", [P, D], F32, 96 + 4 * s) for s in range(2)]
        ln1 = at("ln1", [P, 2, D], F32, 104)
        hT = [at(f"hT{s}", [P, KD, P], F32, 112 + 4 * s) for s in range(2)]
        h = at("h", [P, NT, D], F32, 120)
        RTB = 160
        place = [0]

        def small(name, shape, dt=F32):
            n = 4
            for x in shape[1:]:
                n *= x
            place[0] += (n + 31) // 32 * 32
            return at(name, shape, dt, RTB, place[0] - (n + 31) // 32 * 32)

        st = [small(f"st{s}", [P, 12]) for s in range(3)]
        mv = [small(f"mv{s}", [P, 2]) for s in range(3)]
        sd = [small(f"sd{s}", [P, 2]) for s in range(3)]
        rs = [small(f"rs{s}", [P, 2]) for s in range(3)]
        w_r = small("w_r", [P, KD, 20])
        b_r = small("b_r", [P, 20])
        rc = small("rc", [P, KW - K_THR])
        logit = small("logit", [P, NT, 20])
        gmx = small("gmx", [P, NT])
        ge = small("ge", [P, NT, 4])
        gs = small("gs", [P, NT])
        ga = small("ga", [P, NT, 4])
        gm = small("gm", [P, NT])
        goh = small("goh", [P, NT, 4])
        em = small("em", [P, NT, 4, 4])
        es = small("es", [P, NT, 4])
        v1 = small("v1", [P, NT])
        v2 = small("v2", [P, NT])
        oh = [small(f"oh{s}", [P, NT, 4]) for s in range(2)]
        dv = small("dv", [P, NT])
        wt = small("wt", [P, 2, NT])
        oe = [small(f"oe{s}", [P, NT, 16]) for s in range(2)]
        mm_ = small("mm_", [P, NT, 16])
        pre = small("pre", [P, NT + 1, 16])
        tl = small("tl", [P, 16])
        tl9 = small("tl9", [P, 16, NT])
        inc_ = small("inc_", [P, 16])
        base = small("base", [P, 16])
        pos_e = small("pos_e", [P, NT, 16])
        pos_f = small("pos_f", [P, 2, NT])
        pos_i = small("pos_i", [P, 2, NT], I32)
        eq = small("eq", [P, MT + 1, E - 1])
        et = small("et", [P, MT + 1])
        pack_f = small("pack_f", [P, MT // 2])
        pack = small("pack", [P, MT // 2], I32)
        cum_f = small("cum_f", [P, E])
        cum = small("cum", [P, E], I32)
        assert place[0] <= 11 * KB, place
        w_x = at("w_x", [P, 2, 6144], F32, 0)
        e_hi = [at(f"e_hi{s}", [P, 6144], F32R, 48 + 48 * s) for s in range(2)]
        e_lo = [at(f"e_lo{s}", [P, 6144], F32R, 72 + 48 * s) for s in range(2)]
        hs = [at(f"hs{s}", [P, D], F32, 144 + 4 * s) for s in range(2)]
        ln2 = at("ln2", [P, 2, D], F32, 152)
        hsT_hi = [at(f"hsT_hi{s}", [P, KD, P], F32R, 171 + 8 * s) for s in range(2)]
        hsT_lo = [at(f"hsT_lo{s}", [P, KD, P], F32R, 175 + 8 * s) for s in range(2)]
        y_sb = [at(f"y_sb{s}", [P, D], F32, 187 + 4 * s) for s in range(2)]
        sil = [at(f"sil{s}", [P, F], F32, 195 + s) for s in range(2)]
        hid = [at(f"hid{s}", [P, F], F32, 197 + s) for s in range(2)]
        hidT_hi = [at(f"hidT_hi{s}", [P, 2, P], F32R, 199 + 2 * s) for s in range(2)]
        hidT_lo = [at(f"hidT_lo{s}", [P, 2, P], F32R, 200 + 2 * s) for s in range(2)]
        y0 = [at(f"y0{s}", [P, D], F32, 4 * s) for s in range(3)]
        y1 = [at(f"y1{s}", [P, D], F32, 12 + 4 * s) for s in range(3)]
        ac = [at(f"ac{s}", [P, D], F32, 24 + 4 * s) for s in range(3)]
        h_in = [at(f"h_in{s}", [P, D], F32, 36 + 4 * s) for s in range(3)]

        mT_d = nc.dram_tensor("mT_d", (C * 2, P, T), F32, kind="Internal").ap()
        h_d = nc.dram_tensor("h_d", (T, D), F32, kind="Internal").ap()
        hs_d = nc.dram_tensor("hs_d", (MT * P, D), F32, kind="Internal").ap()
        ys_d = nc.dram_tensor("ys_d", (MT * P, D), F32, kind="Internal").ap()

        s_x = [sem(f"x_landed{i}") for i in range(4)]
        s_const = sem("const_landed")
        s_mask = sem("masks_landed")
        s_w = [sem(f"w_landed{i}") for i in range(3)]
        s_hist = sem("history_landed")
        s_cout = sem("conv_state_stored")
        s_zero = sem("zero_rows_stored")
        s_kv_out = sem("kv_stored")
        s_k = [sem(f"k_landed{i}") for i in range(2)]
        s_v = [sem(f"v_landed{i}") for i in range(2)]
        s_x2 = [sem(f"x_again_landed{i}") for i in range(3)]
        s_m_out = sem("mixed_stored")
        s_wo = [sem(f"wo_landed{i}") for i in range(3)]
        s_m_in = [sem(f"mixed_landed{i}") for i in range(2)]
        s_xn = [sem(f"x_rows_landed{i}") for i in range(2)]
        s_ln1 = sem("out_const_landed")
        s_scat = sem("rows_scattered")
        s_h = sem("h_stored_dram")
        s_hin = [sem(f"h_landed{i}") for i in range(3)]
        s_wg = [sem(f"gate_up_landed{i}") for i in range(2)]
        s_wd = [sem(f"down_landed{i}") for i in range(2)]
        s_hs = [sem(f"rows_landed{i}") for i in range(2)]
        s_ys = [sem(f"expert_rows_stored{i}") for i in range(2)]
        s_ln2 = sem("ln2_landed")
        s_y0 = [sem(f"y0_gathered{i}") for i in range(3)]
        s_y1 = [sem(f"y1_gathered{i}") for i in range(3)]
        s_y = [sem(f"y_stored{i}") for i in range(3)]
        s_apart = [sem(f"apart{i}") for i in range(4)]
        e_mask = sem("masks_ready")
        e_xhi, e_xlo = sem("x_hi_ready"), sem("x_lo_ready")
        e_whi, e_wlo = sem("w_hi_ready"), sem("w_lo_ready")
        e_proj = sem("proj_done")
        e_free = [sem(f"bank_free{n}") for n in range(3)]
        e_vtr, e_vtr_free = sem("v_transposed"), sem("v_rows_ready")
        e_cw = sem("taps_staged")
        e_tap = sem("conv_tap_done")
        e_ptap = sem("pool_tap_done")
        e_pconv = sem("pool_conv_done")
        e_zero = sem("zero_ready")
        e_qd, e_qz, e_vz, e_stage0 = sem("q_d_staged"), sem("q_z_staged"), sem("v_z_staged"), sem("stage_zeroed")
        e_qk, e_sig, e_scan, e_w = sem("z_ready"), sem("sigmoids_ready"), sem("scan_done"), sem("weights_ready")
        e_tr, e_wt, e_av, e_ae = sem("weights_transposed"), sem("wT_ready"), sem("av_done"), sem("attn_stored")
        e_bnd = sem("boundary_ready")
        e_avt, e_dec = sem("stream_transposed"), sem("stream_stored")
        e_ahi, e_alo = sem("attn_hi_ready"), sem("attn_lo_ready")
        e_xhi2, e_xlo2 = sem("x_hi_again"), sem("x_lo_again")
        e_s1, e_cen, e_sq, e_s2 = sem("mean_summed"), sem("centred"), sem("squared"), sem("squares_summed")
        e_var, e_std, e_rstd, e_xhat = sem("var_ready"), sem("std_ready"), sem("rstd_ready"), sem("xhat_ready")
        e_cn, e_chi, e_clo = sem("swish_ready"), sem("c_hi_ready"), sem("c_lo_ready")
        e_w2hi, e_w2lo, e_proj2 = sem("w2_hi_ready"), sem("w2_lo_ready"), sem("mix_proj_done")
        e_free2 = [sem(f"mix_bank_free{n}") for n in range(3)]
        e_m = sem("mixed_ready")
        e_wohi, e_wolo = sem("wo_hi_ready"), sem("wo_lo_ready")
        e_mhi, e_mlo = sem("m_hi_ready"), sem("m_lo_ready")
        e_out, e_r, e_std1, e_rs1 = sem("out_done"), sem("residual_ready"), sem("std1_ready"), sem("rstd1_ready")
        e_st, e_hh = sem("stats_step"), sem("h_stored")
        e_n1, e_g1, e_h = sem("normed_ready"), sem("scaled_ready"), sem("h_ready")
        e_htr, e_hT, e_lg, e_lgs = sem("h_transposed"), sem("hT_ready"), sem("logits_done"), sem("logits_stored")
        e_rt, e_rt_act, e_rank, e_pos, e_te = (sem("route_step"), sem("route_exp"), sem("ranks_done"),
                                              sem("positions_ready"), sem("tile_experts_ready"))
        e_gs = sem("route_gexp")
        e_t, e_rh, e_rl = sem("rows_transposed"), sem("hsT_hi_ready"), sem("hsT_lo_ready")
        e_gh, e_gl = sem("gate_up_hi_ready"), sem("gate_up_lo_ready")
        e_ch, e_cl = sem("down_hi_ready"), sem("down_lo_ready")
        e_gu, e_sil, e_hid, e_t2 = sem("gate_up_done"), sem("silu_ready"), sem("hidden_ready"), sem("hidden_transposed")
        e_hTh, e_hTl = sem("hidT_hi_ready"), sem("hidT_lo_ready")
        e_dn, e_ya = sem("down_done"), sem("y_rows_ready")
        e_c0, e_c1, e_c2, e_cst, e_cstd, e_crs, e_cn2, e_cg, e_y = (
            sem("y0_weighted"), sem("y1_added"), sem("residual2_ready"), sem("stats2_step"), sem("std2_ready"),
            sem("rstd2_ready"), sem("normed2_ready"), sem("scaled2_ready"), sem("y_ready"))

        ds = bass.ds

        def apart(e):
            e.sem_inc({nc.scalar: s_apart[0], nc.vector: s_apart[1], nc.gpsimd: s_apart[2], nc.sync: s_apart[3]}[e], 1)

        def tiles_word(e, i):
            apart(e)
            return e.value_load(pack[0:1, ds(i, 1)], min_val=0, max_val=(1 << 12) - 1)

        def raw_slot(word, place):
            return (word // (1 << (4 * place))) & 1

        def wait_expert(e, landed_, word, place):
            x = (word // (1 << (4 * place))) & (E - 1)
            e.wait_ge(landed_[0], x // 2 * 16 + 16)
            e.wait_ge(landed_[1], ((x + 1) // 2 + (1 >> x)) * 16)

        block = ctx.enter_context(nc.Block())

        SLOT = [0, 1, 0, 1, 2]
        NJ = 5
        PREV = [-3, -2, 0, 1, -1]

        def landed(j, c):
            return 16 * (c + 1) if j == 4 else 16 * (2 * c + (1 if j < 2 else 2))

        def thirds(n):
            return slice(TH * n, TH * (n + 1))

        @block.sync
        def _(e):
            e.dma_start(w_raw[0][:, :], a["w_in"][0]).then_inc(s_w[0], 16)
            for i in range(4):
                part = slice(X_PARTS[i], X_PARTS[i + 1])
                e.dma_start(x_raw[:, part, :], a["xT"][:, part, :]).then_inc(s_x[i], 16)
            e.dma_start(w_raw[1][:, :], a["w_in"][1]).then_inc(s_w[1], 16)
            e.dma_start(ident[:, :], a["consts"][:, K_ID:K_ID + P]).then_inc(s_const, 16)
            e.dma_start(tri[:, :], a["consts"][:, K_TRI:K_TRI + P]).then_inc(s_const, 16)
            e.dma_start(ones[:, :], a["consts"][:, K_ONE:K_ONE + P]).then_inc(s_const, 16)
            e.dma_start(cw[:, :, :], a["conv"]).then_inc(s_const, 16)
            e.dma_start(lngb[:, :, :], a["conv_ln"]).then_inc(s_const, 16)
            e.dma_start(bg[:, :], a["b_gate"]).then_inc(s_const, 16)
            e.dma_start(mask_raw[:, :], a["consts"][:, K_CM:K_CM + P * (1 + NB)]).then_inc(s_mask, 16)
            e.wait_ge(e_zero, 1)

            def load_round(c, first):
                for j in range(first, NJ):
                    e.wait_ge(e_whi, c * NJ + (NJ + PREV[j] + 1))
                    e.wait_ge(e_wlo, c * NJ + (NJ + PREV[j] + 1))
                    e.dma_start(w_raw[SLOT[j]][:, :], a["w_in"][ds(c * NJ + j, 1), :, :].rearrange(
                        "a p n -> p (a n)")).then_inc(s_w[SLOT[j]], 16)

            def zero_rows(i, n):
                e.dma_start(hs_d.rearrange("(p r) (h n) -> p r h n", p=P, h=2)[:, ds(i, 1), n, :].rearrange(
                    "p r n -> p (r n)"), zero[:, :]).then_inc(s_zero, 16)

            load_round(0, 2)
            with e.Fori(1, C) as c:
                load_round(c, 0)
                for i in range(MT // 3):
                    zero_rows(c * (MT // 3) + (i - MT // 3), 0)
                    zero_rows(c * (MT // 3) + (i - MT // 3), 1)

            e.wait_ge(e_proj, 15 + 15 * C)

            def load_half(rd, i, stream, half, first=False):
                s = i % 2
                before = DEC[(i + 2) % 4] + (0 if i >= 2 else -NI)
                if not first:
                    e.wait_ge(e_qk, rd * NI + before + 1)
                    apart(e)
                e.dma_start(k_in[s][:, :, :], a["cache_k"][ds(rd * 2 + stream, 1), half, :, :].rearrange(
                    "a p n -> p (a n)").rearrange("p (c n) -> p c n", c=4)).then_inc(s_k[s], 16)
                if not first:
                    e.wait_ge(e_av, rd * NI + before + 1)
                e.dma_start(v_in[s][:, :, :], a["cache_v"][ds(rd * 2 + stream, 1), half, :, :].rearrange(
                    "a p n -> p (a n)").rearrange("p (c n) -> p c n", n=512)).then_inc(s_v[s], 16)

            load_half(0, 0, 0, 1, first=True)
            load_half(0, 1, 0, 0, first=True)
            e.wait_ge(e_free[0], NJ * C)
            e.wait_ge(e_free[1], NJ * C)
            e.wait_ge(e_free[2], NJ * C)
            e.wait_ge(e_vtr_free, 3 * C)
            e.dma_start(a["k_out"], kT[:, :, :]).then_inc(s_kv_out, 16)
            e.dma_start(a["v_out"][0:NPR, :].rearrange("(b p) n -> p b n", p=P), v_p[:, :, :]).then_inc(s_kv_out, 16)
            e.dma_start(a["v_out"][NPR:T, :], v_s[:, :]).then_inc(s_kv_out, 16)
            with e.Fori(0, ROUNDS - 1) as rd:
                load_half(rd, 2, 1, 1)
                load_half(rd, 3, 1, 0)
                load_half(rd + 1, 0, 0, 1)
                load_half(rd + 1, 1, 0, 0)
            load_half(ROUNDS - 1, 2, 1, 1)
            load_half(ROUNDS - 1, 3, 1, 0)

            def load_mix(c, j):
                e.dma_start(w_raw[j][:, :], a["w_mix"][ds(c * 3 + j, 1), :, :].rearrange("a p n -> p (a n)")).then_inc(s_w[j], 16)

            e.wait_ge(s_kv_out, 48)
            e.wait_ge(e_vz, ROUNDS)
            for k in range(KD):
                if k >= 3:
                    e.wait_ge(e_xhi2, k - 2)
                    e.wait_ge(e_xlo2, k - 2)
                e.dma_start(x_raw2[k % 3][:, :], a["xT"][:, k, :]).then_inc(s_x2[k % 3], 16)
            e.wait_ge(e_av, NI * ROUNDS)
            for j in range(3):
                load_mix(0, j)
            with e.Fori(1, C * 2) as c:
                for j in range(3):
                    e.wait_ge(e_w2hi, c * 3 + (j - 2))
                    e.wait_ge(e_w2lo, c * 3 + (j - 2))
                    load_mix(c, j)

            def load_wo(k):
                e.dma_start(w_raw[k % 3][:, :], a["w_out"][k]).then_inc(s_wo[k % 3], 16)

            def load_tile(t, s):
                e.dma_start(m_raw[s][:, :, :], mT_d[:, :, ds(t * P, P)].rearrange("k p n -> p k n")).then_inc(s_m_in[s], 16)
                e.dma_start(x_n[s][:, :], a["x_rows"][ds(t * P, P), :]).then_inc(s_xn[s], 16)

            e.wait_ge(e_w2hi, 3 * 2 * C)
            e.wait_ge(e_w2lo, 3 * 2 * C)
            for k in range(3):
                load_wo(k)
            for k in range(3, KD):
                e.wait_ge(e_wohi, k - 2)
                e.wait_ge(e_wolo, k - 2)
                load_wo(k)
            e.wait_ge(e_proj2, 12 * 2 * C)
            e.wait_ge(s_m_out, 16 * 2 * C)
            load_tile(0, 0)
            e.dma_start(ln1[:, :, :], a["ln1"]).then_inc(s_ln1, 16)
            e.dma_start(w_r[:, :, :], a["w_router"]).then_inc(s_ln1, 16)
            e.dma_start(b_r[:, :], a["b_router"]).then_inc(s_ln1, 16)
            e.dma_start(rc[:, :], a["consts"][:, K_THR:KW]).then_inc(s_ln1, 16)
            load_tile(1, 1)
            with e.Fori(0, 3) as i:
                for s in range(2):
                    e.wait_ge(e_mlo, i * 2 + (s + 1))
                    e.wait_ge(e_r, i * 2 + (s + 1))
                    load_tile(i * 2 + (s + 2), s)
            e.wait_ge(e_mlo, 7)
            e.wait_ge(e_r, 7)
            load_tile(8, 0)

            def load_rows(i, s):
                e.dma_start(hs[s][:, :], hs_d[ds(i * P, P), :]).then_inc(s_hs[s], 16)

            def store_rows(i, s):
                e.wait_ge(e_ya, i + 1)
                e.dma_start(ys_d[ds(i * P, P), :], y_sb[s][:, :]).then_inc(s_ys[s], 16)

            e.wait_ge(s_h, 16 * NT)
            e.wait_ge(s_scat, 16 * 2 * NT)
            for s in range(2):
                load_rows(s, s)
            e.dma_start(ln2[:, :, :], a["ln2"]).then_inc(s_ln2, 16)

            def rows_step(t, s, store=True):
                e.wait_ge(e_t, t + 1)
                load_rows(t + 2, s)
                if store:
                    store_rows(t - 2, s)

            rows_step(0, 0, store=False)
            rows_step(1, 1, store=False)
            with e.Fori(1, (MT - 3) // 2) as i:
                for s in range(2):
                    rows_step(i * 2 + s, s)
            rows_step(MT - 3, 0)
            for t in range(MT - 4, MT - 1):
                store_rows(t, t % 2)

            def load_h(t, s):
                e.dma_start(h_in[s][:, :], h_d[ds(t * P, P), :]).then_inc(s_hin[s], 16)

            e.wait_ge(e_cl, MT + 1)
            for s in range(3):
                load_h(s, s)
            store_rows(MT - 1, 0)

            with e.Fori(0, NT // 3 - 1) as i:
                for s in range(3):
                    e.wait_ge(e_c2, i * 3 + (s + 1))
                    load_h(i * 3 + (s + 3), s)
                    e.wait_ge(e_y, i * 3 + (s + 1))
                    e.dma_start(a["y_out"][ds(i * (3 * P) + s * P, P), :], ac[s][:, :]).then_inc(s_y[s], 16)
            for s in range(3):
                e.wait_ge(e_y, NT - 2 + s)
                e.dma_start(a["y_out"][(NT - 3 + s) * P:(NT - 2 + s) * P, :], ac[s][:, :]).then_inc(s_y[s], 16)
            for s in range(3):
                e.wait_ge(s_y[s], 16 * (NT // 3))
            e.wait_ge(s_cout, 32 * C)

        @block.tensor
        def _(e):
            def split_product(outs, w_parts, x_parts, start, stop):
                whi, wlo = w_parts
                xhi, xlo = x_parts
                e.matmul(outs, whi, xhi, start=start, stop=False)
                e.matmul(outs, whi, xlo, start=False, stop=False)
                return e.matmul(outs, wlo, xhi, start=False, stop=stop)

            e.sem_inc(e_proj, 15)
            e.wait_ge(e_xlo, KD)

            def project(c):
                for j in range(NJ):
                    s = SLOT[j]
                    e.wait_ge(e_wlo, c * NJ + (NJ + j + 1))
                    for n in range(3):
                        if j or later(c, 1):
                            e.wait_ge(e_free[n], c * NJ + j)
                        for k in range(KD):
                            m = split_product(bank[n][:, 0:TH],
                                              (w_hi[s][:, k * P:(k + 1) * P], w_lo[s][:, k * P:(k + 1) * P]),
                                              (x_hi[:, k, thirds(n)], x_lo[:, k, thirds(n)]), k == 0, k == KD - 1)
                        m.then_inc(e_proj, 1)
                    if j == 3:
                        for n in range(3):
                            e.wait_ge(e_free[n], c * NJ + 3)
                        if later(c, 1):
                            e.wait_ge(e_vtr_free, c * 3)
                        else:
                            e.wait_ge(s_const, 96)
                        for b in range(NT):
                            tgt = zb[0][:, 128 * b:128 * (b + 1)] if b < 8 else zb[1][:, 0:128]
                            m = e.transpose(tgt, vT[:, b * P:(b + 1) * P], ident[:, :])
                            if b in (3, 7, 8):
                                m.then_inc(e_vtr, 1)

            project(0)
            with e.Fori(1, C) as c:
                project(c)

            def scores(rd, m):
                item = ITEMS[m % NI]
                m0 = m % NI
                z = zb[m % 2]
                if m >= 2:
                    e.wait_ge(e_sig, rd * NI + (m - 1))
                if item[0] == "d":
                    i = DEC.index(m0)
                    up = m // NI
                    e.wait_ge(s_k[i % 2], rd * 32 + 16 * (2 * up + i // 2 + 1))
                    e.wait_ge(e_qd, rd * 2 + (2 * up + item[1] + 1))
                    if item[2] == 1:
                        nz = bank[0][:, 0:P]
                        if rd is not None and (m >= NI or item[1] or later(rd, 1)):
                            e.wait_ge(e_dec, rd * 2 + (2 * up + item[1]))
                        e.matmul(nz, ident_b[:, :], smask[:, ds(rd * 2 + (2 * up + item[1]), 1), :].rearrange(
                            "p a n -> p (a n)"), start=True, stop=False, skip_group_check=True)
                        for p in range(4):
                            e.matmul(bank[0][32 * p:32 * p + 32, 0:P], q_d[item[1]][:, p, :], kT[:, p, NPR:T],
                                     start=False, stop=True, skip_group_check=True)
                    for n in range(2):
                        for p in range(4):
                            mm = e.matmul(z[32 * p:32 * p + 32, 512 * n:512 * n + 512], q_d[item[1]][:, p, :],
                                          k_in[i % 2][:, p, 512 * n:512 * n + 512], start=True, stop=True)
                else:
                    _, t, hh = item
                    w = width(item)
                    e.wait_ge(e_qz, rd + (1 + m // NI))
                    for lo in range(0, w, 512):
                        hi = min(lo + 512, w)
                        mm = e.matmul(z[:, lo:hi], q_z[:, hh, t * P:(t + 1) * P],
                                      kT[:, ds(rd + m // NI, 1), lo:hi].rearrange("p a n -> p (a n)"),
                                      start=True, stop=hi < w, skip_group_check=True)
                    mm = e.matmul(z[:, w - P:w], ident_b[:, :], cmask[:, :], start=False, stop=True,
                                  skip_group_check=True)
                mm.then_inc(e_qk, 1)

            def transposes(rd, m):
                item = ITEMS[m]
                off = HALF + P - width(item)
                e.wait_ge(e_w, rd * NI + (m + 1))
                for g, blocks in enumerate(groups(item)):
                    n = GRP0[m] + g
                    if n >= 2 or later(rd, 1):
                        e.wait_ge(e_wt, rd * NGRP + (n - 1 if n >= 2 else 0))
                    for b in blocks:
                        mm = e.transpose(bank[1 + n % 2][:, P * (b % 4):P * (b % 4 + 1)],
                                         sig[m % 2][:, off + b * P:off + (b + 1) * P], ident[:, :])
                    mm.then_inc(e_tr, 1)

            def values(rd, m):
                item = ITEMS[m]
                nb = width(item) // P
                if m or later(rd, 1):
                    e.wait_ge(e_ae, rd * NI + m)
                e.wait_ge(e_wt, rd * NGRP + GRP0[m + 1])
                if item[0] == "d":
                    i = DEC.index(m)
                    e.wait_ge(s_v[i % 2], rd * 32 + 16 * (i // 2 + 1))
                    for b in range(nb):
                        for p in range(4):
                            rhs = v_in[i % 2][:, b, P * p:P * (p + 1)] if b < 8 else v_s[:, P * p:P * (p + 1)]
                            mm = e.matmul(bank7[32 * p:32 * p + 32, 0:P], wT[m % 2][:, b, 32 * p:32 * p + 32], rhs,
                                          start=b == 0 and item[2] == 1, stop=b == nb - 1 and item[2] == 0,
                                          skip_group_check=True)
                else:
                    _, t, hh = item
                    e.wait_ge(e_vz, rd + 1)
                    for b in range(nb):
                        mm = e.matmul(bank7[HD * hh:HD * hh + HD, 0:P], v_z[:, b, HD * hh:HD * hh + HD],
                                      wT[m % 2][:, b, :], start=(b == 0), stop=(b == nb - 1))
                mm.then_inc(e_av, 1)

            def stream_transpose(rd, m):
                e.wait_ge(e_ae, rd * NI + (m + 1))
                e.transpose(bank[0][:, P:2 * P], av_sb[:, :], ident[:, :]).then_inc(e_avt, 1)

            def att_round(rd, last):
                for m in range(NI):
                    transposes(rd, m)
                    if m - 1 in DEC_OLD:
                        stream_transpose(rd, m - 1)
                    if m + 2 < NI or not last:
                        scores(rd, m + 2)
                    values(rd, m)

            for n in range(3):
                e.wait_ge(e_free[n], NJ * C)
            e.wait_ge(e_vtr_free, 3 * C)
            e.wait_ge(e_mask, 3)
            scores(0, 0)
            scores(0, 1)
            att_round(0, False)
            with e.Fori(1, ROUNDS - 1) as rd:
                att_round(rd, False)
            att_round(ROUNDS - 1, True)

            def channel_sums(signal, step=None):
                for n in range(3):
                    if step is not None:
                        e.wait_ge(step, n + 1)
                    for c in range(C):
                        m = e.matmul(cn_sum[n], ones[:, :], cT[:, c, thirds(n)] if step is None else sq[:, c, :],
                                     start=c == 0, stop=c == C - 1)
                    m.then_inc(signal, 1)

            e.wait_ge(e_sig, NI * ROUNDS)
            channel_sums(e_s1)

            def mix(c):
                for j in range(4):
                    s = min(j, 2)
                    if j < 3:
                        e.wait_ge(e_w2lo, c * 3 + (s + 1))
                    if j == 2:
                        e.wait_ge(e_alo, C)
                    if j == 3:
                        e.wait_ge(e_clo, C)
                    for n in range(3):
                        if j or later(c, 1):
                            e.wait_ge(e_free2[n], c * 4 + j)
                        for k in range(KD if j < 2 else 4):
                            kk = k + 4 * (j == 3)
                            rhs = ((x_hi, x_lo), (x_hi, x_lo), (a_hi, a_lo), (c_hi, c_lo))[j]
                            m = split_product(bank[n][:, 0:TH],
                                              (w_hi[s][:, kk * P:(kk + 1) * P], w_lo[s][:, kk * P:(kk + 1) * P]),
                                              (rhs[0][:, k, thirds(n)], rhs[1][:, k, thirds(n)]),
                                              k == 0, k == (KD if j < 2 else 4) - 1)
                        m.then_inc(e_proj2, 1)
                    if not later(c, 1) and j == 0:
                        channel_sums(e_s2, e_sq)

            e.wait_ge(e_wt, NGRP * ROUNDS)
            e.wait_ge(e_dec, 2 * ROUNDS)
            e.wait_ge(e_xlo2, KD)
            mix(0)
            with e.Fori(1, 2 * C) as c:
                mix(c)

            def out_tile(t, s, first=False):
                e.wait_ge(e_mlo, t + 1)
                if later(t, 2):
                    e.wait_ge(e_r, t - 1)
                for k in range(KD):
                    if first:
                        e.wait_ge(e_wolo, k + 1)
                    for n in range(2):
                        m = split_product(zb[s][:, 512 * n:512 * n + 512], (m_hi[s][:, k, :], m_lo[s][:, k, :]),
                                          (wo_hi[:, k, 512 * n:512 * n + 512], wo_lo[:, k, 512 * n:512 * n + 512]),
                                          k == 0, k == KD - 1)
                m.then_inc(e_out, 1)

            def h_transposes(t, s):
                e.wait_ge(e_h, t + 1)
                if later(t, 1):
                    e.wait_ge(e_hT, t * 2)
                for k in range(KD):
                    m = e.transpose(bank[k // 4][:, P * (k % 4):P * (k % 4 + 1)], r[s][:, k * P:(k + 1) * P], ident[:, :])
                m.then_inc(e_htr, 1)

            def router(t, s):
                e.wait_ge(e_hT, t * 2 + 2)
                if later(t, 1):
                    e.wait_ge(e_lgs, t)
                for k in range(KD):
                    m = e.matmul(bank[2][:, 0:20], hT[s][:, k, :], w_r[:, k, :], start=k == 0, stop=k == KD - 1)
                m.then_inc(e_lg, 1)

            for n in range(3):
                e.wait_ge(e_free2[n], 4 * 2 * C)
            out_tile(0, 0, first=True)
            e.wait_ge(s_ln1, 64)
            out_tile(1, 1)
            h_transposes(0, 0)
            for t in range(2):
                out_tile(t + 2, t)
                router(t, t)
                h_transposes(t + 1, 1 - t)
            with e.Fori(1, 3) as i:
                for s in range(2):
                    t = i * 2 + (s + 2)
                    out_tile(t, s)
                    router(i * 2 + s, s)
                    h_transposes(i * 2 + (s + 1), 1 - s)
            out_tile(8, 0)
            router(6, 0)
            h_transposes(7, 1)
            router(7, 1)
            h_transposes(8, 0)
            router(8, 0)

            e.wait_ge(e_rt, RT_RANK)
            e.matmul(bank7[:, 0:NT * 16], tri[:, :], mm_[:, :, :].rearrange("p t e -> p (t e)"), start=True, stop=False)
            e.matmul(bank7[:, 0:NT * 16], ones[:, :], pre[:, 0:NT, :].rearrange("p t e -> p (t e)"), start=False, stop=True)
            e.matmul(zb[1][:, 0:16], ones[:, :], pre[:, NT, :], start=True, stop=True).then_inc(e_rank, 1)

            def rows_t(t, s, n=0):
                e.wait_ge(s_hs[s], n * 16 + 16)
                if later(t, 1):
                    e.wait_ge(e_rl, t)
                for k in range(KD):
                    m = e.transpose(zb[1][:, P * k:P * (k + 1)], hs[s][:, k * P:(k + 1) * P], ident[:, :])
                m.then_inc(e_t, 1)

            def gate_up(t, s):
                e.wait_ge(e_rl, t + 1)
                if later(t, 2):
                    e.wait_ge(e_hid, t - 1)
                for k in range(KD):
                    if k % 4 == 0:
                        e.wait_ge(e_gl, t * 2 + (3 + k // 4))
                    m = split_product(bank[1 + s][:, :], (hsT_hi[s][:, k, :], hsT_lo[s][:, k, :]),
                                      (e_hi[s][:, 512 * k:512 * (k + 1)], e_lo[s][:, 512 * k:512 * (k + 1)]),
                                      k == 0, k == KD - 1)
                m.then_inc(e_gu, 1)

            def hidden_t(t, s):
                e.wait_ge(e_hid, t + 1)
                if later(t, 1):
                    e.wait_ge(e_hTl, t)
                for k in range(2):
                    m = e.transpose(bank7[:, P * k:P * (k + 1)], hid[s][:, P * k:P * (k + 1)], ident[:, :])
                m.then_inc(e_t2, 1)

            def down(t, s):
                e.wait_ge(e_hTl, t + 1)
                e.wait_ge(e_cl, t + 2)
                if later(t, 1):
                    e.wait_ge(e_ya, t)
                for n in range(2):
                    for k in range(2):
                        o = 4096 + 1024 * k + 512 * n
                        m = split_product(zb[0][:, 512 * n:512 * (n + 1)], (hidT_hi[s][:, k, :], hidT_lo[s][:, k, :]),
                                          (e_hi[s][:, o:o + 512], e_lo[s][:, o:o + 512]), k == 0, k == 1)
                m.then_inc(e_dn, 1)

            e.wait_ge(e_pos, 1)
            e.wait_ge(e_lgs, NT)
            rows_t(0, 0)
            rows_t(1, 1)
            gate_up(0, 0)
            hidden_t(0, 0)
            for t in (1, 2):
                rows_t(t + 1, 1 - t % 2, 1)
                gate_up(t, t % 2)
                down(t - 1, 1 - t % 2)
                hidden_t(t, t % 2)
            with e.Fori(1, (MT - 3) // 2) as i:
                for u_ in range(2):
                    t = i * 2 + (u_ + 1)
                    rows_t(i * 2 + (u_ + 2), u_, i + 1)
                    gate_up(t, 1 - u_)
                    down(i * 2 + u_, u_)
                    hidden_t(t, 1 - u_)
            rows_t(MT - 1, 0, MT // 2)
            gate_up(MT - 2, 1)
            down(MT - 3, 0)
            hidden_t(MT - 2, 1)
            gate_up(MT - 1, 0)
            down(MT - 2, 1)
            hidden_t(MT - 1, 0)
            down(MT - 1, 0)

        @block.scalar
        def _(e):
            e.sem_inc(e_whi, NJ)

            def split_hi(c, j):
                e.wait_ge(s_w[SLOT[j]], landed(j, c))
                e.wait_ge(e_proj, c * 15 + (15 + 3 * (PREV[j] + 1)))
                e.activation(w_hi[SLOT[j]][:, :], w_raw[SLOT[j]][:, :], ACT.Copy).then_inc(e_whi, 1)

            def round_(c, last):
                for j in range(NJ):
                    if j + 1 < NJ:
                        split_hi(c, j + 1)
                    elif not last:
                        split_hi(c + 1, 0)
                    if j == 3:
                        for n in range(3):
                            e.wait_ge(e_proj, c * 15 + (15 + 3 * j + n + 1))
                            e.activation(qT[:, ds(c, 1), thirds(n)].rearrange("p a n -> p (a n)"), bank[n][:, 0:TH],
                                         ACT.Copy).then_inc(e_free[n], 1)
                        for n in range(3):
                            e.wait_ge(e_vtr, c * 3 + (n + 1))
                            if n < 2:
                                src = zb[0][:, 512 * n:512 * (n + 1)].rearrange("p (b n) -> p b n", n=P)
                                dst = v_p[:, 4 * n:4 * n + 4, ds(c * P, P)]
                            else:
                                src, dst = zb[1][:, 0:P], v_s[:, ds(c * P, P)]
                            e.activation(dst, src, ACT.Copy).then_inc(e_vtr_free, 1)
                    elif j == 4:
                        for n in range(3):
                            e.wait_ge(e_proj, c * 15 + (15 + 3 * j + n + 1))
                            e.activation(kT[:, ds(c, 1), thirds(n)].rearrange("p a n -> p (a n)"), bank[n][:, 0:TH],
                                         ACT.Copy).then_inc(e_free[n], 1)
                    elif j in (0, 2):
                        if j == 0 and later(c, 1):
                            e.wait_ge(e_pconv, c)
                        for n in range(3):
                            e.wait_ge(e_proj, c * 15 + (15 + 3 * j + n + 1))
                            e.activation((sg if j == 0 else vT)[:, thirds(n)], bank[n][:, 0:TH],
                                         ACT.Sigmoid if j == 0 else ACT.Copy).then_inc(e_free[n], 1)

            split_hi(0, 0)
            for k in range(KD):
                e.wait_ge(s_x[sum(k >= x for x in X_PARTS[1:])], 16)
                e.activation(x_hi[:, k, :], x_raw[:, k, :], ACT.Copy).then_inc(e_xhi, 1)
            round_(0, False)
            with e.Fori(1, C - 1) as c:
                round_(c, False)
            round_(C - 1, True)

            def sigmoids(rd, m):
                item = ITEMS[m % NI]
                w = width(item)
                off = HALF + P - w
                s = m % 2
                e.wait_ge(e_qk, rd * NI + (m + 1))
                if m >= 2:
                    e.wait_ge(e_w, rd * NI + (m - 1))
                    e.wait_ge(e_tr, rd * NGRP + GRP0[m - 1])
                parts = [(bank[0][:, 0:P], HALF, P)] if item[0] == "d" and item[2] == 1 else []
                wz = HALF if item[0] == "d" else w
                parts.append((zb[s][:, 0:wz], off, wz))
                for src, o, n in parts:
                    e.activation(keep[s][:, o:o + n], src, ACT.Sigmoid, scale=-SCALE)
                    i = e.activation(sig[s][:, o:o + n], src, ACT.Sigmoid, scale=SCALE)
                i.then_inc(e_sig, 1)

            def x_again_hi(k):
                e.wait_ge(s_x2[k % 3], 16 * (k // 3 + 1))
                e.activation(x_hi[:, k, :], x_raw2[k % 3][:, :], ACT.Copy).then_inc(e_xhi2, 1)

            def attn_hi(c):
                if c == 0:
                    e.wait_ge(e_qz, ROUNDS)
                e.wait_ge(e_ae, NI * c + NI)
                e.wait_ge(e_dec, 2 * ROUNDS)
                e.activation(a_hi[:, c, :], attnT[:, c, :], ACT.Copy).then_inc(e_ahi, 1)

            def copies(rd, m):
                if m > 1 or later(rd, 1):
                    e.wait_ge(e_av, rd * NI + max(m - 1, 0))
                for g, blocks in enumerate(groups(ITEMS[m])):
                    n = GRP0[m] + g
                    e.wait_ge(e_tr, rd * NGRP + (n + 1))
                    e.activation(wT[m % 2][:, blocks[0]:blocks[-1] + 1, :],
                                 bank[1 + n % 2][:, 0:P * len(blocks)].rearrange("p (b n) -> p b n", n=P),
                                 ACT.Copy).then_inc(e_wt, 1)

            def att_round(rd, last):
                for m in range(NI):
                    if m + 1 < NI or not last:
                        sigmoids(rd, m + 1)
                    copies(rd, m)
                    if last:
                        if m in TAIL_X:
                            x_again_hi(TAIL_X.index(m))
                        if m in TAIL_A:
                            attn_hi(TAIL_A.index(m))

            sigmoids(0, 0)
            att_round(0, False)
            with e.Fori(1, ROUNDS - 1) as rd:
                att_round(rd, False)
            att_round(ROUNDS - 1, True)

            W0 = [16 * 2 * C, 16 * 2 * C, 16 * C]

            def split2_hi(c, j, first=False):
                e.wait_ge(s_w[j], c * 16 + (W0[j] + 16))
                if not first:
                    e.wait_ge(e_proj2, c * 12 - (12 - (3, 6, 12)[j]))
                e.activation(w_hi[j][:, :], w_raw[j][:, :], ACT.Copy).then_inc(e_w2hi, 1)

            def gate(c, j):
                for n in range(3):
                    e.wait_ge(e_proj2, c * 12 + (3 * j + n + 1))
                    apart(e)
                    e.activation((sg_a, sg_b)[j][:, thirds(n)], bank[n][:, 0:TH], ACT.Sigmoid,
                                 bias=bg[:, ds(c * 2 + j, 1)]).then_inc(e_free2[n], 1)

            def mix(c, last):
                e.wait_ge(e_m, c)
                for j in range(2):
                    gate(c, j)
                    if not last:
                        split2_hi(c + 1, j)
                if not last:
                    split2_hi(c + 1, 2)

            for k in (6, 7):
                x_again_hi(k)
            attn_hi(3)
            split2_hi(0, 0, first=True)
            split2_hi(0, 1, first=True)
            for n in range(3):
                e.wait_ge(e_cen, n + 1)
                if n == 0:
                    e.wait_ge(e_xlo2, KD)
                else:
                    e.wait_ge(e_s2, n)
                e.activation(sq[:, :, :], cT[:, :, thirds(n)], ACT.Square).then_inc(e_sq, 1)
            split2_hi(0, 2, first=True)
            e.wait_ge(e_alo, C)
            gate(0, 0)
            split2_hi(1, 0)
            for n in range(3):
                e.wait_ge(e_var, n + 1)
                e.activation(rstd_c[:, thirds(n)], rstd_c[:, thirds(n)], ACT.Sqrt).then_inc(e_std, 1)
            for c in range(C):
                e.wait_ge(e_xhat, c + 1)
                e.activation(cT[:, c, :], cT[:, c, :], ACT.Silu, scale=lngb[:, 0, c:c + 1],
                             bias=lngb[:, 1, c:c + 1]).then_inc(e_cn, 1)
                e.wait_ge(e_cn, c + 1)
                e.activation(c_hi[:, c, :], cT[:, c, :], ACT.Copy).then_inc(e_chi, 1)
            gate(0, 1)
            split2_hi(1, 1)
            split2_hi(1, 2)
            with e.Fori(1, 2 * C - 1) as c:
                mix(c, False)
            mix(2 * C - 1, True)

            e.wait_ge(e_proj2, 12 * 2 * C - 6)
            for k in range(KD):
                e.wait_ge(s_wo[k % 3], 16 * (k // 3 + 1))
                e.activation(wo_hi[:, k, :], w_raw[k % 3][:, :], ACT.Copy).then_inc(e_wohi, 1)

            def split_m(t, s, i=0):
                e.wait_ge(s_m_in[s], i * 16 + 16)
                if later(t, 2):
                    e.wait_ge(e_out, t - 1)
                e.activation(m_hi[s][:, :, :], m_raw[s][:, :, :], ACT.Copy).then_inc(e_mhi, 1)

            def std_and_norm(t, s):
                e.wait_ge(e_st, t * 3 + 3)
                e.activation(sd[s][:, 0:1], mv[s][:, 1:2], ACT.Sqrt).then_inc(e_std1, 1)
                e.wait_ge(e_g1, t + 1)
                e.wait_ge(e_rs1, t + 1)
                e.activation(r[s][:, :], r[s][:, :], ACT.Copy, scale=rs[s][:, 0:1]).then_inc(e_n1, 1)

            def copy_hT(t, s):
                e.wait_ge(e_htr, t + 1)
                for k in range(2):
                    e.activation(hT[s][:, 4 * k:4 * k + 4, :], bank[k][:, :].rearrange("p (b n) -> p b n", n=P),
                                 ACT.Copy).then_inc(e_hT, 1)
                e.activation(h[:, ds(t, 1), :].rearrange("p a n -> p (a n)"), r[s][:, :], ACT.Copy).then_inc(e_hh, 1)

            split_m(0, 0)
            split_m(1, 1)
            split_m(2, 0, 1)
            std_and_norm(0, 0)
            with e.Fori(0, 3) as i:
                for s in range(2):
                    split_m(i * 2 + (s + 3), 1 - s, i + (1 + s))
                    copy_hT(i * 2 + s, s)
                    std_and_norm(i * 2 + (s + 1), 1 - s)
            copy_hT(6, 0)
            std_and_norm(7, 1)
            copy_hT(7, 1)
            std_and_norm(8, 0)
            copy_hT(8, 0)

            e.wait_ge(e_rt, RT_GEXP)
            e.activation(ge[:, :, :], ge[:, :, :], ACT.Exp).then_inc(e_gs, 1)
            e.wait_ge(e_rt, RT_DV)
            e.activation(dv[:, :], dv[:, :], ACT.Exp).then_inc(e_rt_act, 1)

            def rows_hi(t, s):
                e.wait_ge(e_t, t + 1)
                if later(t, 2):
                    e.wait_ge(e_gu, t - 1)
                e.activation(hsT_hi[s][:, :, :], zb[1][:, :].rearrange("p (b n) -> p b n", n=P), ACT.Copy).then_inc(e_rh, 1)

            def piece_hi(t, s, lo, signal, slot):
                e.activation(e_hi[s][:, lo:lo + 2048], w_x[:, ds(slot, 1), lo:lo + 2048].rearrange("p a n -> p (a n)"),
                             ACT.Copy).then_inc(signal, 1)

            def gate_up_hi(t, s, word, place):
                wait_expert(e, s_wg, word, place)
                piece_hi(t, s, 0, e_gh, raw_slot(word, place))

            def gate_up_hi2(t, s, word, place):
                piece_hi(t, s, 2048, e_gh, raw_slot(word, place))

            def down_hi(t, s, word, place):
                if later(t, 2):
                    e.wait_ge(e_dn, t - 1)
                wait_expert(e, s_wd, word, place)
                piece_hi(t, s, 4096, e_ch, raw_slot(word, place))

            def silu(t, s):
                e.wait_ge(e_gu, t + 1)
                if later(t, 2):
                    e.wait_ge(e_hid, t - 1)
                e.activation(sil[s][:, :], bank[1 + s][:, 0:F], ACT.Silu).then_inc(e_sil, 1)

            def hidden_hi(t, s):
                e.wait_ge(e_t2, t + 1)
                if later(t, 2):
                    e.wait_ge(e_dn, t - 1)
                e.activation(hidT_hi[s][:, :, :], bank7[:, 0:F].rearrange("p (b n) -> p b n", n=P), ACT.Copy).then_inc(e_hTh, 1)

            def copy_y(t, s, n=0):
                e.wait_ge(e_dn, t + 1)
                if later(t, 2):
                    e.wait_ge(s_ys[s], n * 16)
                e.activation(y_sb[s][:, :], zb[0][:, :], ACT.Copy).then_inc(e_ya, 1)

            def moe_step(t, s, down_at, gate_at, n=0, first=False):
                if gate_at is not None:
                    rows_hi(t + 1, 1 - s)
                down_hi(t, s, *down_at)
                if gate_at is not None:
                    gate_up_hi(t + 1, 1 - s, *gate_at)
                silu(t, s)
                if gate_at is not None:
                    gate_up_hi2(t + 1, 1 - s, *gate_at)
                if not first:
                    copy_y(t - 1, 1 - s, n)
                hidden_hi(t, s)

            def word_last(e):
                return tiles_word(e, MT // 2 - 1)

            e.wait_ge(e_te, 1)
            word = tiles_word(e, 0)
            gate_up_hi(0, 0, word, 0)
            gate_up_hi2(0, 0, word, 0)
            rows_hi(0, 0)
            moe_step(0, 0, (word, 0), (word, 1), first=True)
            moe_step(1, 1, (word, 1), (word, 2))
            word = tiles_word(e, 1)
            moe_step(2, 0, (word, 0), (word, 1))
            moe_step(3, 1, (word, 1), (word, 2), 1)
            with e.Fori(2, MT // 2) as i:
                word = tiles_word(e, i)
                for u_ in range(2):
                    moe_step(i * 2 + u_, u_, (word, u_), (word, u_ + 1), i - 1 + u_)
            moe_step(MT - 1, 0, (word_last(e), 2), None, MT // 2 - 1)
            copy_y(MT - 1, 0, MT // 2)

            def weight0(t, s, n=0):
                e.wait_ge(s_y0[s], n * 16 + 16)
                if later(t, 3):
                    e.wait_ge(s_y[s], n * 16)
                e.activation(ac[s][:, :], y0[s][:, :], ACT.Copy, scale=wt[:, 0, ds(t, 1)]).then_inc(e_c0, 1)

            def std_and_norm2(t, s):
                e.wait_ge(e_cst, t * 3 + 3)
                e.activation(sd[s][:, 0:1], mv[s][:, 1:2], ACT.Sqrt).then_inc(e_cstd, 1)
                e.wait_ge(e_cg, t + 1)
                e.wait_ge(e_crs, t + 1)
                e.activation(ac[s][:, :], ac[s][:, :], ACT.Copy, scale=rs[s][:, 0:1]).then_inc(e_cn2, 1)

            e.wait_ge(e_dn, MT)
            weight0(0, 0)
            weight0(1, 1)
            std_and_norm2(0, 0)
            weight0(2, 2)
            std_and_norm2(1, 1)
            with e.Fori(1, NT // 3) as i:
                for s in range(3):
                    weight0(i * 3 + s, s, i)
                    std_and_norm2(i * 3 + (s - 1), (s - 1) % 3)
            std_and_norm2(NT - 1, 2)

        @block.vector
        def _(e):
            def tt(out, x, y, op):
                return e.tensor_tensor(out, x, y, op)

            e.sem_inc(e_wlo, NJ)
            e.memset(u[:, 0:HIST], 0.0)

            def split_lo(c, j):
                e.wait_ge(e_whi, c * NJ + (NJ + j + 1))
                s = SLOT[j]
                tt(w_lo[s][:, :], w_raw[s][:, :], w_hi[s][:, :].bitcast(F32), ALU.subtract).then_inc(e_wlo, 1)

            def taps(c, lo, hi):
                o = cT[:, ds(c, 1), 0:NPR].rearrange("p a n -> p (a n)")
                os_ = cT[:, ds(c, 1), NPR:T].rearrange("p a (b w) -> p (a b) w", w=NST)
                if lo == 0:
                    e.wait_ge(e_cw, c + 1)
                    e.wait_ge(s_hist, c * 16 + 16)
                for k in range(lo, hi):
                    for out, src, n, before in ((o, u[:, k:k + NPR], tap_no(k, 0), tap_no(k - 1, 0)),
                                                (os_, u_s[:, :, k:k + NST], tap_no(k, 1), tap_no(k - 1, 1))):
                        if n is None:
                            continue
                        if k == 0:
                            i = e.tensor_scalar(out, src, cwc[:, 0:1], cwc[:, CK:CK + 1], ALU.mult, ALU.add)
                        else:
                            e.wait_ge(e_tap, c * NTAP + (before + 1))
                            i = e.scalar_tensor_tensor(out=out, in0=src, scalar=cwc[:, k:k + 1], in1=out,
                                                       op0=ALU.mult, op1=ALU.add)
                        i.then_inc(e_tap, 1)
                if hi == CK:
                    e.wait_ge(e_pconv, c + 1)
                    e.wait_ge(e_tap, c * NTAP + (NTAP - 1))
                    tt(o, o, pacc[:, :], ALU.add).then_inc(e_tap, 1)

            def round_(c, last):
                split_lo(c, 1)
                split_lo(c, 2)
                if later(c, 1):
                    e.wait_ge(e_pconv, c)
                    e.wait_ge(s_cout, c * 32)
                    e.wait_ge(e_tap, c * NTAP)
                for n in range(3):
                    e.wait_ge(e_proj, c * 15 + (15 + 3 + n + 1))
                    np_ = TH if n < 2 else NPR - 2 * TH
                    i = tt(u[:, HIST + TH * n:HIST + TH * n + np_], bank[n][:, 0:np_], sg[:, TH * n:TH * n + np_], ALU.mult)
                    if n == 2:
                        i = tt(u_s[:, :, HIST:USW], bank[n][:, np_:TH].rearrange("p (b w) -> p b w", w=NST),
                               sg[:, NPR:T].rearrange("p (b w) -> p b w", w=NST), ALU.mult)
                    i.then_inc(e_free[n], 1)
                e.wait_ge(e_free[2], c * NJ + 2)
                taps(c, 0, 7)
                split_lo(c, 3)
                taps(c, 7, 14)
                split_lo(c, 4)
                taps(c, 14, 24)
                if not last:
                    split_lo(c + 1, 0)
                taps(c, 24, CK)

            split_lo(0, 0)
            for k in range(KD):
                e.wait_ge(e_xhi, k + 1)
                tt(x_lo[:, k, :], x_raw[:, k, :], x_hi[:, k, :].bitcast(F32), ALU.subtract).then_inc(e_xlo, 1)
            e.wait_ge(e_mask, 2)
            round_(0, False)
            with e.Fori(1, C - 1) as c:
                round_(c, False)
            round_(C - 1, True)

            W = HALF + P

            def scan(rd, m):
                item = ITEMS[m % NI]
                s = m % 2
                off = W - width(item)
                old = item[0] == "d" and item[2] == 0
                e.wait_ge(e_sig, rd * NI + (m + 1))
                if old:
                    e.wait_ge(e_w, rd * NI + m)
                    i = e.tensor_copy(keep[s][:, W:W + 1], carry[:, :])
                else:
                    i = e.memset(keep[s][:, W:W + 1], 1.0)
                i.then_inc(e_bnd, 1)
                e.wait_ge(e_bnd, rd * NI + (m + 1))
                rev = keep[s][:, off:W][:, ::-1]
                e.tensor_tensor_scan(rev, rev, rev, carry[:, :] if old else 1.0, ALU.mult, ALU.bypass).then_inc(e_scan, 1)
                e.wait_ge(e_scan, rd * NI + (m + 1))
                if item[0] == "d" and item[2] == 1:
                    e.tensor_copy(carry[:, :], keep[s][:, off:off + 1])
                tt(sig[s][:, off:W], sig[s][:, off:W], keep[s][:, off + 1:W + 1], ALU.mult).then_inc(e_w, 1)

            def store(rd, m):
                item = ITEMS[m]
                if item[0] == "d" and item[2] == 1:
                    e.sem_inc(e_ae, 1)
                    return
                e.wait_ge(e_av, rd * NI + (m + 1))
                if item[0] == "p":
                    _, t, hh = item
                    rows = slice(HD * hh, HD * hh + HD)
                    i = e.tensor_copy(attnT[rows, ds(rd, 1), t * P:(t + 1) * P].rearrange("p a n -> p (a n)"), bank7[rows, 0:P])
                else:
                    i = e.tensor_copy(av_sb[:, :], bank7[:, 0:P])
                i.then_inc(e_ae, 1)

            def store_stream(rd, stream):
                e.wait_ge(e_avt, rd * 2 + (stream + 1))
                av = bank[0][:, P:2 * P].rearrange("p (c w) -> p c w", w=32)
                for hh in range(2):
                    rows = slice(HD * hh, HD * hh + HD)
                    i = e.tensor_copy(attnT[rows, :, ds(rd * (2 * NST) + (NPR + NST * stream), NST)],
                                      av[rows, :, NST * hh:NST * hh + NST])
                i.then_inc(e_dec, 1)

            def x_again_lo(k):
                e.wait_ge(e_xhi2, k + 1)
                tt(x_lo[:, k, :], x_raw2[k % 3][:, :], x_hi[:, k, :].bitcast(F32), ALU.subtract).then_inc(e_xlo2, 1)

            def attn_lo(c):
                e.wait_ge(e_ahi, c + 1)
                tt(a_lo[:, c, :], attnT[:, c, :], a_hi[:, c, :].bitcast(F32), ALU.subtract).then_inc(e_alo, 1)

            def att_round(rd, last):
                for m in range(NI):
                    if m + 1 < NI or not last:
                        scan(rd, m + 1)
                    if m - 1 in DEC_OLD:
                        store_stream(rd, ITEMS[m - 1][1])
                    store(rd, m)
                    if last:
                        if m in TAIL_X:
                            x_again_lo(TAIL_X.index(m))
                        if m in TAIL_A:
                            attn_lo(TAIL_A.index(m))

            e.wait_ge(e_pconv, C)
            e.wait_ge(s_cout, 32 * C)
            e.wait_ge(e_tap, C * NTAP)
            scan(0, 0)
            with e.Fori(0, ROUNDS - 1) as rd:
                att_round(rd, False)
            att_round(ROUNDS - 1, True)

            def split2_lo(c, j):
                e.wait_ge(e_w2hi, c * 3 + (j + 1))
                tt(w_lo[j][:, :], w_raw[j][:, :], w_hi[j][:, :].bitcast(F32), ALU.subtract).then_inc(e_w2lo, 1)

            def wo_low(k):
                e.wait_ge(e_wohi, k + 1)
                tt(wo_lo[:, k, :], w_raw[k % 3][:, :], wo_hi[:, k, :].bitcast(F32), ALU.subtract).then_inc(e_wolo, 1)

            def mix(c, last, first=False):
                if not last and not first:
                    split2_lo(c + 1, 0)
                if not last:
                    split2_lo(c + 1, 1)
                for j in range(2):
                    if last:
                        for k in range(4 * j, 4 * j + 4):
                            wo_low(k)
                    for n in range(3):
                        e.wait_ge(e_proj2, c * 12 + (3 * (j + 2) + n + 1))
                        o = (sg_a, sg_b)[j][:, thirds(n)]
                        tt(o, bank[n][:, 0:TH], o, ALU.mult).then_inc(e_free2[n], 1)
                if not last:
                    split2_lo(c + 1, 2)

            for k in (6, 7):
                x_again_lo(k)
            attn_lo(3)
            split2_lo(0, 0)
            split2_lo(0, 1)
            for n in range(3):
                e.wait_ge(e_s1, n + 1)
                for c in range(C):
                    i = e.scalar_tensor_tensor(out=cT[:, c, thirds(n)], in0=cn_sum[n], scalar=-1.0 / 512,
                                               in1=cT[:, c, thirds(n)], op0=ALU.mult, op1=ALU.add)
                i.then_inc(e_cen, 1)
            split2_lo(0, 2)
            for n in range(3):
                e.wait_ge(e_s2, n + 1)
                e.tensor_scalar(rstd_c[:, thirds(n)], cn_sum[n], 1.0 / 512, EPS, ALU.mult, ALU.add).then_inc(e_var, 1)
            e.wait_ge(e_std, 3)
            e.reciprocal(rstd_c[:, :], rstd_c[:, :]).then_inc(e_rstd, 1)
            e.wait_ge(e_rstd, 1)
            for c in range(C):
                tt(cT[:, c, :], cT[:, c, :], rstd_c[:, :], ALU.mult).then_inc(e_xhat, 1)
            split2_lo(1, 0)
            for c in range(C):
                e.wait_ge(e_chi, c + 1)
                tt(c_lo[:, c, :], cT[:, c, :], c_hi[:, c, :].bitcast(F32), ALU.subtract).then_inc(e_clo, 1)
            mix(0, False, first=True)
            with e.Fori(1, 2 * C - 1) as c:
                mix(c, False)
            mix(2 * C - 1, True)

            def split_m(t, s):
                e.wait_ge(e_mhi, t + 1)
                tt(m_lo[s][:, :, :], m_raw[s][:, :, :], m_hi[s][:, :, :].bitcast(F32), ALU.subtract).then_inc(e_mlo, 1)

            def stats(x, s, step, n0):
                e.bn_stats(st[s][:, 0:6], x[:, 0:512])
                e.bn_stats(st[s][:, 6:12], x[:, 512:1024]).then_inc(step, 1)
                e.wait_ge(step, n0 + 1)
                apart(e)
                e.bn_aggr(mv[s][:, :], st[s][:, :]).then_inc(step, 1)
                e.wait_ge(step, n0 + 2)
                e.tensor_scalar(mv[s][:, 1:2], mv[s][:, 1:2], EPS, None, ALU.add).then_inc(step, 1)

            def residual(t, s, i=0):
                e.wait_ge(e_out, t + 1)
                e.wait_ge(s_xn[s], i * 16 + 16)
                if later(t, 2):
                    e.wait_ge(e_htr, t - 1)
                    e.wait_ge(e_hh, t - 1)
                e.scalar_tensor_tensor(out=r[s][:, :], in0=x_n[s][:, :], scalar=ALPHA, in1=zb[s][:, :],
                                       op0=ALU.mult, op1=ALU.add).then_inc(e_r, 1)
                e.wait_ge(e_r, t + 1)
                stats(r[s], s, e_st, t * 3)
                e.scalar_tensor_tensor(out=r[s][:, :], in0=r[s][:, :], scalar=mv[s][:, 0:1], in1=ln1[:, 0, :],
                                       op0=ALU.subtract, op1=ALU.mult).then_inc(e_g1, 1)
                e.wait_ge(e_std1, t + 1)
                e.reciprocal(rs[s][:, 0:1], sd[s][:, 0:1]).then_inc(e_rs1, 1)

            def store_logits(t):
                e.wait_ge(e_lg, t + 1)
                tt(logit[:, ds(t, 1), :].rearrange("p a n -> p (a n)"), bank[2][:, 0:20], b_r[:, :], ALU.add).then_inc(e_lgs, 1)

            split_m(0, 0)
            split_m(1, 1)
            residual(0, 0)
            split_m(2, 0)
            for t in range(2):
                residual(t + 1, 1 - t, t)
                split_m(t + 3, 1 - t)
                store_logits(t)
            with e.Fori(1, 3) as i:
                for s in range(2):
                    residual(i * 2 + (s + 1), 1 - s, i + s)
                    split_m(i * 2 + (s + 3), 1 - s)
                    store_logits(i * 2 + s)
            residual(7, 1, 3)
            store_logits(6)
            residual(8, 0, 4)
            store_logits(7)
            store_logits(8)

            step = [0]

            def link(i):
                step[0] += 1
                i.then_inc(e_rt, 1)
                e.wait_ge(e_rt, step[0])

            def over(x, n):
                return x.rearrange("p (m o) -> p m o", o=1).to_broadcast([P, x.shape[1], n])

            def first_max(src, mx, score, best, out):
                link(e.tensor_reduce(mx, src, AX.X, ALU.max))
                link(tt(score, src, over(mx, 4), ALU.is_equal))
                link(tt(score, score, rc[:, K_FIRST - K_THR:K_FIRST - K_THR + 4].rearrange("p (o m) -> p o m", o=1)
                        .to_broadcast([P, NT, 4]), ALU.mult))
                link(e.tensor_reduce(best, score, AX.X, ALU.max))
                link(tt(out, score, over(best, 4), ALU.is_equal))

            e.wait_ge(e_lgs, NT)
            lg = logit[:, :, 0:4]
            first_max(lg, gmx[:, :], ga[:, :, :], gm[:, :], goh[:, :, :])
            link(tt(ge[:, :, :], lg, over(gmx[:, :], 4), ALU.subtract))
            assert step[0] == RT_GEXP
            link(tt(em[:, :, :, :], logit[:, :, 4:20].rearrange("p t (g j) -> p t g j", g=4),
                    goh[:, :, :].rearrange("p t (g o) -> p t g o", o=1).to_broadcast([P, NT, 4, 4]), ALU.mult))
            link(e.tensor_reduce(es[:, :, :], em[:, :, :, :].rearrange("p t g j -> p t j g"), AX.X, ALU.add))
            first_max(es[:, :, :], v1[:, :], ga[:, :, :], gm[:, :], oh[0][:, :, :])
            link(e.scalar_tensor_tensor(out=es[:, :, :], in0=oh[0][:, :, :], scalar=NEG, in1=es[:, :, :],
                                        op0=ALU.mult, op1=ALU.add))
            first_max(es[:, :, :], v2[:, :], ga[:, :, :], gm[:, :], oh[1][:, :, :])
            link(tt(dv[:, :], v2[:, :], v1[:, :], ALU.subtract))
            assert step[0] == RT_DV, step
            for k in range(2):
                link(tt(oe[k][:, :, :].rearrange("p t (g j) -> p t g j", g=4),
                        goh[:, :, :].rearrange("p t (g o) -> p t g o", o=1).to_broadcast([P, NT, 4, 4]),
                        oh[k][:, :, :].rearrange("p t (o j) -> p t o j", o=1).to_broadcast([P, NT, 4, 4]), ALU.mult))
            link(tt(mm_[:, :, :], oe[0][:, :, :], oe[1][:, :, :], ALU.add))
            link(e.memset(pre[:, 0, :], 0.0))
            for t in range(NT):
                link(tt(pre[:, t + 1, :], pre[:, t, :], mm_[:, t, :], ALU.add))
            assert step[0] == RT_RANK, step
            e.wait_ge(e_gs, 1)
            link(e.tensor_reduce(gs[:, :], ge[:, :, :], AX.X, ALU.add))
            link(e.reciprocal(gs[:, :], gs[:, :]))
            e.wait_ge(e_rt_act, 1)
            link(e.tensor_scalar(v1[:, :], dv[:, :], 1.0, None, ALU.add))
            link(e.reciprocal(v1[:, :], v1[:, :]))
            link(tt(wt[:, 0, :], v1[:, :], gs[:, :], ALU.mult))
            link(tt(wt[:, 1, :], wt[:, 0, :], dv[:, :], ALU.mult))
            e.wait_ge(e_rank, 1)
            link(tt(tl9[:, :, :], zb[1][:, 0:16].rearrange("p (m o) -> p m o", o=1).to_broadcast([P, 16, NT]),
                    rc[:, 0:NT].rearrange("p (o m) -> p o m", o=1).to_broadcast([P, 16, NT]), ALU.is_gt))
            link(e.tensor_reduce(tl[:, :], tl9[:, :, :], AX.X, ALU.add))
            link(e.tensor_tensor_scan(inc_[:, :], tl[:, :], tl[:, :], 0.0, ALU.add, ALU.bypass))
            link(tt(base[:, :], inc_[:, :], tl[:, :], ALU.subtract))
            link(e.tensor_scalar(base[:, :], base[:, :], float(P), None, ALU.mult))
            link(tt(pos_e[:, :, :], bank7[:, 0:NT * 16].rearrange("p (t m) -> p t m", t=NT),
                    base[:, :].rearrange("p (o m) -> p o m", o=1).to_broadcast([P, NT, 16]), ALU.add))
            for k in range(2):
                link(tt(oe[k][:, :, :], oe[k][:, :, :], pos_e[:, :, :], ALU.mult))
                link(e.tensor_reduce(pos_f[:, k, :], oe[k][:, :, :], AX.X, ALU.add))
            e.tensor_copy(pos_i[:, :, :], pos_f[:, :, :]).then_inc(e_pos, 1)
            link(tt(eq[:, :, :], rc[:, K_TILE - K_THR:K_FIRST - K_THR].rearrange("p (m o) -> p m o", o=1)
                    .to_broadcast([P, MT + 1, E - 1]),
                    inc_[:, 0:E - 1].rearrange("p (o m) -> p o m", o=1).to_broadcast([P, MT + 1, E - 1]), ALU.is_ge))
            link(e.tensor_reduce(et[:, :], eq[:, :, :], AX.X, ALU.add))

            def every_second(x, first, n):
                return x[:, first:first + 2 * n].rearrange("p (m o) -> p m o", o=2)[:, :, 0]

            n = MT // 2
            link(e.scalar_tensor_tensor(out=pack_f[:, :], in0=every_second(et, 1, n), scalar=16.0,
                                        in1=every_second(et, 0, n), op0=ALU.mult, op1=ALU.add))
            link(e.scalar_tensor_tensor(out=pack_f[:, :], in0=every_second(et, 2, n), scalar=256.0, in1=pack_f[:, :],
                                        op0=ALU.mult, op1=ALU.add))
            link(e.tensor_scalar(cum_f[:, :], inc_[:, :], 1.0, None, ALU.add))
            link(e.tensor_copy(cum[:, :], cum_f[:, :]))
            e.tensor_copy(pack[:, :], pack_f[:, :]).then_inc(e_te, 1)

            def rows_lo(t, s):
                e.wait_ge(e_rh, t + 1)
                if later(t, 2):
                    e.wait_ge(e_gu, t - 1)
                tt(hsT_lo[s][:, :, :], zb[1][:, :].rearrange("p (b n) -> p b n", n=P), hsT_hi[s][:, :, :].bitcast(F32),
                   ALU.subtract).then_inc(e_rl, 1)

            def piece_lo(s, lo, signal, slot):
                tt(e_lo[s][:, lo:lo + 2048], w_x[:, ds(slot, 1), lo:lo + 2048].rearrange("p a n -> p (a n)"),
                   e_hi[s][:, lo:lo + 2048].bitcast(F32), ALU.subtract).then_inc(signal, 1)

            def gate_up_lo(t, s, p, slot):
                e.wait_ge(e_gh, t * 2 + (p + 1))
                piece_lo(s, 2048 * p, e_gl, slot)

            def down_lo(t, s, slot):
                e.wait_ge(e_ch, t + 1)
                if later(t, 2):
                    e.wait_ge(e_dn, t - 1)
                piece_lo(s, 4096, e_cl, slot)

            def hidden(t, s):
                e.wait_ge(e_sil, t + 1)
                if later(t, 2):
                    e.wait_ge(e_t2, t - 1)
                tt(hid[s][:, :], sil[s][:, :], bank[1 + s][:, F:2 * F], ALU.mult).then_inc(e_hid, 1)

            def hidden_lo(t, s):
                e.wait_ge(e_hTh, t + 1)
                if later(t, 2):
                    e.wait_ge(e_dn, t - 1)
                tt(hidT_lo[s][:, :, :], bank7[:, 0:F].rearrange("p (b n) -> p b n", n=P), hidT_hi[s][:, :, :].bitcast(F32),
                   ALU.subtract).then_inc(e_hTl, 1)

            def moe_step(t, s, down_slot, gate_slot):
                if gate_slot is not None:
                    rows_lo(t + 1, 1 - s)
                down_lo(t, s, down_slot)
                hidden(t, s)
                if gate_slot is not None:
                    gate_up_lo(t + 1, 1 - s, 0, gate_slot)
                    gate_up_lo(t + 1, 1 - s, 1, gate_slot)
                hidden_lo(t, s)

            e.sem_inc(e_gl, 2)
            e.sem_inc(e_cl, 1)
            e.wait_ge(e_te, 1)
            word = tiles_word(e, 0)
            gate_up_lo(0, 0, 0, raw_slot(word, 0))
            gate_up_lo(0, 0, 1, raw_slot(word, 0))
            rows_lo(0, 0)
            moe_step(0, 0, raw_slot(word, 0), raw_slot(word, 1))
            moe_step(1, 1, raw_slot(word, 1), raw_slot(word, 2))
            with e.Fori(1, MT // 2) as i:
                word = tiles_word(e, i)
                for u_ in range(2):
                    moe_step(i * 2 + u_, u_, raw_slot(word, u_), raw_slot(word, u_ + 1))
            moe_step(MT - 1, 0, raw_slot(tiles_word(e, MT // 2 - 1), 2), None)

            def combine(t, s, n=0):
                e.wait_ge(e_c0, t + 1)
                e.wait_ge(s_y1[s], n * 16 + 16)
                e.scalar_tensor_tensor(out=ac[s][:, :], in0=y1[s][:, :], scalar=wt[:, 1, ds(t, 1)], in1=ac[s][:, :],
                                       op0=ALU.mult, op1=ALU.add).then_inc(e_c1, 1)
                e.wait_ge(e_c1, t + 1)
                e.wait_ge(s_hin[s], n * 16 + 16)
                e.scalar_tensor_tensor(out=ac[s][:, :], in0=h_in[s][:, :], scalar=ALPHA, in1=ac[s][:, :],
                                       op0=ALU.mult, op1=ALU.add).then_inc(e_c2, 1)
                e.wait_ge(e_c2, t + 1)
                stats(ac[s], s, e_cst, t * 3)
                e.scalar_tensor_tensor(out=ac[s][:, :], in0=ac[s][:, :], scalar=mv[s][:, 0:1], in1=ln2[:, 0, :],
                                       op0=ALU.subtract, op1=ALU.mult).then_inc(e_cg, 1)

            def rstd2(t, s):
                e.wait_ge(e_cstd, t + 1)
                e.reciprocal(rs[s][:, 0:1], sd[s][:, 0:1]).then_inc(e_crs, 1)

            e.wait_ge(s_ln2, 16)
            with e.Fori(0, NT // 3) as i:
                for s in range(3):
                    combine(i * 3 + s, s, i)
                    rstd2(i * 3 + s, s)

        @block.gpsimd
        def _(e):
            e.memset(zero[:, :], 0.0).then_inc(e_zero, 1)
            e.wait_ge(s_mask, 16)
            e.tensor_copy(cmask[:, :], mask_raw[:, 0:P]).then_inc(e_mask, 1)
            e.tensor_copy(smask[:, :, :], mask_raw[:, P:].rearrange("p (b n) -> p b n", n=P)).then_inc(e_mask, 1)
            e.wait_ge(s_const, 96)
            e.tensor_copy(ident_b[:, :], ident[:, :]).then_inc(e_mask, 1)
            n_p = CK - DVE_TAPS
            NPT = 2 * n_p - 2
            prod = sg[:, 0:NPR]

            def pool_taps(c):
                if later(c, 1):
                    e.wait_ge(e_tap, c * NTAP)
                e.tensor_copy(cwc[:, :], cw[:, ds(c, 1), :].rearrange("p a n -> p (a n)")).then_inc(e_cw, 1)
                if later(c, 1):
                    e.wait_ge(s_cout, c * 32)
                e.dma_start(u_s[:, :, 0:HIST], a["hist"][ds(c, 1), :, :, :].rearrange("a p b w -> p (a b) w")).then_inc(s_hist, 16)
                e.wait_ge(e_cw, c + 1)
                e.wait_ge(e_free[2], c * NJ + 2)
                e.wait_ge(s_hist, c * 16 + 16)
                e.dma_start(a["conv_out"][ds(c, 1), :, 0, :].rearrange("a p w -> p (a w)"),
                            u[:, NPR:NPR + HIST]).then_inc(s_cout, 16)
                e.dma_start(a["conv_out"][ds(c, 1), :, 1:1 + NB, :].rearrange("a p b w -> p (a b) w"),
                            u_s[:, :, NST:USW]).then_inc(s_cout, 16)
                n = 0
                for k in range(DVE_TAPS, CK):
                    if n:
                        e.wait_ge(e_ptap, c * NPT + n)
                        apart(e)
                    i = e.tensor_scalar(prod if n else pacc[:, :], u[:, k:k + NPR], cwc[:, k:k + 1], None, ALU.mult)
                    i.then_inc(e_ptap, 1)
                    n += 1
                    if n > 1:
                        e.wait_ge(e_ptap, c * NPT + n)
                        apart(e)
                        i = e.tensor_tensor(pacc[:, :], pacc[:, :], prod, ALU.add)
                        i.then_inc(e_ptap if k < CK - 1 else e_pconv, 1)
                        n += 1
                assert n == NPT + 1

            pool_taps(0)
            with e.Fori(1, C) as c:
                pool_taps(c)

            for n in range(3):
                e.wait_ge(e_free[n], NJ * C)
            e.wait_ge(e_proj, 15 + 15 * C)
            e.wait_ge(e_wlo, NJ + NJ * C)
            e.wait_ge(e_vtr_free, 3 * C)
            e.memset(q_z[:, :, :], 0.0).then_inc(e_stage0, 1)
            e.memset(q_d[0][:, :, :], 0.0).then_inc(e_stage0, 1)
            e.memset(q_d[1][:, :, :], 0.0).then_inc(e_stage0, 1)
            e.wait_ge(e_stage0, 3)

            def stage_q_d(rd, a_):
                for hh in range(2):
                    rows = slice(HD * hh, HD * hh + HD)
                    i = e.tensor_copy(q_d[a_][rows, :, NST * hh:NST * hh + NST],
                                      qT[rows, :, ds(rd * (2 * NST) + (NPR + NST * a_), NST)])
                i.then_inc(e_qd, 1)

            def stage_q_z(rd):
                for hh in range(2):
                    rows = slice(HD * hh, HD * hh + HD)
                    i = e.tensor_copy(q_z[rows, hh, :], qT[rows, ds(rd, 1), 0:NPR].rearrange("p a n -> p (a n)"))
                i.then_inc(e_qz, 1)

            def stage_v_z(rd):
                e.wait_ge(e_qz, rd + 1)
                e.tensor_copy(v_z[:, :, :], v_p[:, :, ds(rd * P, P)]).then_inc(e_vz, 1)

            stage_q_d(0, 0)
            stage_q_z(0)
            stage_v_z(0)
            e.wait_ge(e_vz, 1)
            stage_q_d(0, 1)
            with e.Fori(0, ROUNDS - 1) as rd:
                e.wait_ge(e_vz, rd + 1)
                e.wait_ge(e_qk, rd * NI + (DEC[1] + 1))
                stage_q_d(rd + 1, 0)
                e.wait_ge(e_qk, rd * NI + (DEC[3] + 1))
                stage_q_d(rd + 1, 1)
                e.wait_ge(e_qk, rd * NI + NI)
                stage_q_z(rd + 1)
                e.wait_ge(e_av, rd * NI + NI)
                stage_v_z(rd + 1)

            def mixed(c):
                for n in range(3):
                    e.wait_ge(e_free2[n], c * 4 + 4)
                if later(c, 1):
                    e.wait_ge(s_m_out, c * 16)
                e.tensor_tensor(m_sb[:, :], sg_a[:, :], sg_b[:, :], ALU.add).then_inc(e_m, 1)
                e.wait_ge(e_m, c + 1)
                e.dma_start(mT_d[ds(c, 1), :, :].rearrange("a p n -> p (a n)"), m_sb[:, :]).then_inc(s_m_out, 16)

            mixed(0)
            with e.Fori(1, 2 * C) as c:
                mixed(c)

            def add_b(t, s):
                e.wait_ge(e_n1, t + 1)
                e.tensor_tensor(r[s][:, :], r[s][:, :], ln1[:, 1, :], ALU.add).then_inc(e_h, 1)

            def store_h(t):
                e.wait_ge(e_hh, t + 1)
                e.dma_start(h_d[ds(t * P, P), :], h[:, ds(t, 1), :].rearrange("p a n -> p (a n)")).then_inc(s_h, 16)

            add_b(0, 0)
            with e.Fori(0, 4) as i:
                for s in range(2):
                    add_b(i * 2 + (s + 1), 1 - s)
                    store_h(i * 2 + s)
            store_h(8)

            e.wait_ge(e_out, NT)
            for p in range(2):
                e.dma_start(w_x[:, p, 0:4096], a["w_exp"][p][:, 0:4096]).then_inc(s_wg[p], 16)
                e.dma_start(w_x[:, p, 4096:], a["w_exp"][p][:, 4096:]).then_inc(s_wd[p], 16)

            e.wait_ge(e_pos, 1)
            e.wait_ge(s_zero, 16 * 2 * MT)
            e.wait_ge(e_hh, NT)
            for t in range(NT):
                for k in range(2):
                    e.indirect_dma_start(hs_d[:, :], bass.IndirectOffsetOnAxis(ap=pos_i[:, k, t:t + 1], axis=0),
                                         h[:, t, :], None).then_inc(s_scat, 16)

            e.wait_ge(e_te, 1)
            with e.Fori(1, E // 2) as q:
                used = [e.value_load(cum[0:1, ds(q * 2 + (p - 2), 1)], min_val=1, max_val=MT + 1) for p in range(2)]
                for p in range(2):
                    expert = a["w_exp"][ds(q * 2 + p, 1), :, :].rearrange("a p n -> p (a n)")
                    e.wait_ge(e_gl, used[p] * 2)
                    e.wait_ge(s_wg[p], q * 16)
                    e.dma_start(w_x[:, p, 0:4096], expert[:, 0:4096]).then_inc(s_wg[p], 16)
                    e.wait_ge(e_cl, used[p])
                    e.wait_ge(s_wd[p], q * 16)
                    e.dma_start(w_x[:, p, 4096:], expert[:, 4096:]).then_inc(s_wd[p], 16)
            for p in range(2):
                e.wait_ge(s_wg[p], 16 * (E // 2))
                e.wait_ge(s_wd[p], 16 * (E // 2))

            def gather(t, s):
                for k, (y, sm) in enumerate(((y0, s_y0), (y1, s_y1))):
                    e.indirect_dma_start(y[s][:, :], None, ys_d[:, :],
                                         bass.IndirectOffsetOnAxis(ap=pos_i[:, k, t:t + 1], axis=0)).then_inc(sm[s], 16)

            def add_b2(t, s):
                e.wait_ge(e_cn2, t + 1)
                e.tensor_tensor(ac[s][:, :], ac[s][:, :], ln2[:, 1, :], ALU.add).then_inc(e_y, 1)

            e.wait_ge(s_ys[0], 16 * (MT // 2 + 1))
            e.wait_ge(s_ys[1], 16 * (MT // 2))
            e.wait_ge(e_dn, MT)
            for t in range(3):
                gather(t, t)
            for t in range(NT):
                add_b2(t, t % 3)
                if t + 3 < NT:
                    gather(t + 3, t % 3)


def _consts(np):
    k = np.zeros((P, KW), np.float32)
    i = np.arange(P)
    k[:, K_ID:K_ID + P] = np.eye(P)
    k[:, K_TRI:K_TRI + P] = i[:, None] < i[None, :]
    k[:, K_ONE:K_ONE + P] = 1
    k[:, K_CM:K_CM + P] = np.where(i[None, :] < i[:, None], 0, NEG)
    b, j = i // NST, i % NST
    for n in range(NB):
        seen = (b[None, :] == n) & (j[None, :] < j[:, None])
        k[:, K_SM + n * P:K_SM + (n + 1) * P] = np.where(seen, 0, NEG)
    k[:, K_THR:K_THR + NT] = P * np.arange(NT)
    k[:, K_TILE:K_TILE + MT + 1] = np.arange(MT + 1)
    k[:, K_FIRST:K_FIRST + EG] = EG - np.arange(EG)
    return k


def kernel(x_prompt, x_sample, cache_k, cache_v, state_conv, w_in, w_branch_attn, w_branch_conv, conv_w, conv_b,
           conv_ln_g, conv_ln_b, w_gate, b_gate, w_out, ln1_g, ln1_b, w_router_group, b_router_group, w_router_expert,
           b_router_expert, w_expert_gate, w_expert_up, w_expert_down, ln2_g, ln2_b):
    import numpy as np
    from concourse import bacc
    from concourse.bass_utils import run_bass_kernel_spmd

    def arr(x):
        return np.asarray(x)

    def chunks(w):
        k, n = w.shape
        return w.reshape(k // P, P, n // P, P).transpose(2, 1, 0, 3).reshape(n // P, P, k)

    def rows(v, n=P):
        return np.broadcast_to(v, (n, *v.shape))

    x_rows = np.concatenate([arr(x_prompt)[0], arr(x_sample).reshape(NSA, D)], 0)
    wi = chunks(arr(w_in)[0]).reshape(5, C, P, D)
    w_in_u = np.stack([wi[4], wi[3], wi[2], wi[0], wi[1]], 1).reshape(5 * C, P, D)
    wg = chunks(arr(w_gate)[0]).reshape(2, 2 * C, P, D)
    wb = np.concatenate([chunks(arr(w_branch_attn)[0]), chunks(arr(w_branch_conv)[0])], 2)
    w_mix = np.stack([wg[0], wg[1], wb], 1).reshape(6 * C, P, D)
    gu = np.concatenate([arr(w_expert_gate)[0], arr(w_expert_up)[0]], 2).reshape(E, KD, P, 2 * F)
    dn = arr(w_expert_down)[0].reshape(E, 2, P, D)
    w_exp = np.concatenate([gu.transpose(0, 2, 1, 3).reshape(E, P, KD * 2 * F),
                            dn.transpose(0, 2, 1, 3).reshape(E, P, 2 * D)], 2)
    conv = np.concatenate([arr(conv_w)[0].T.reshape(C, P, CK), arr(conv_b)[0].reshape(C, P, 1)], 2).transpose(1, 0, 2)
    ins = {
        "xT": x_rows.T.reshape(KD, P, T).transpose(1, 0, 2),
        "x_rows": x_rows,
        "w_in": w_in_u,
        "w_mix": w_mix,
        "w_out": arr(w_out)[0].reshape(KD, P, D),
        "w_exp": w_exp,
        "consts": _consts(np),
        "conv": conv,
        "conv_ln": np.stack([arr(conv_ln_g)[0].reshape(C, P).T, arr(conv_ln_b)[0].reshape(C, P).T], 1),
        "b_gate": arr(b_gate)[0].reshape(2, 2 * C, P).transpose(2, 1, 0).reshape(P, 4 * C),
        "ln1": rows(np.stack([arr(ln1_g)[0], arr(ln1_b)[0]])),
        "ln2": rows(np.stack([arr(ln2_g)[0], arr(ln2_b)[0]])),
        "w_router": np.concatenate([arr(w_router_group)[0], arr(w_router_expert)[0]], 1).reshape(KD, P, 20).transpose(1, 0, 2),
        "b_router": rows(np.concatenate([arr(b_router_group)[0], arr(b_router_expert)[0]])),
        "cache_k": arr(cache_k)[0].reshape(NB, 2, HALF, C, P).transpose(0, 1, 4, 3, 2).reshape(NB, 2, P, C * HALF),
        "cache_v": arr(cache_v)[0].reshape(NB, 2, HALF // P, P, 512).transpose(0, 1, 3, 2, 4).reshape(NB, 2, P, -1),
        "hist": arr(state_conv)[0].reshape(NB, HIST, C, P).transpose(2, 3, 0, 1),
    }
    outs = {
        "y_out": (T, D), "k_out": (P, C, T), "v_out": (T, 512), "conv_out": (C, P, 1 + NB, HIST),
    }
    nc = bacc.Bacc("TRN2", target_bir_lowering=False, num_devices=1)
    a = {}
    for n, x in ins.items():
        ins[n] = np.ascontiguousarray(x)
        a[n] = nc.dram_tensor(n, ins[n].shape, mybir.dt.from_np(ins[n].dtype), kind="ExternalInput").ap()
    for n, shape in outs.items():
        a[n] = nc.dram_tensor(n, shape, F32, kind="ExternalOutput").ap()
    encoder_layer(nc, a)
    got = run_bass_kernel_spmd(nc, [ins], core_ids=[0]).results[0]

    y = got["y_out"]
    k = got["k_out"].transpose(2, 1, 0).reshape(T, 8, HD)
    v = got["v_out"].reshape(T, 8, HD)
    cv = got["conv_out"].transpose(2, 3, 0, 1).reshape(1 + NB, HIST, 512)
    return (y[None, :NPR], y[NPR:].reshape(NB, NST, D),
            k[None, None, :NPR], v[None, None, :NPR], cv[None, :1],
            k[NPR:].reshape(1, NB, NST, 8, HD), v[NPR:].reshape(1, NB, NST, 8, HD), cv[None, 1:])
```
